# Optimizing a Trainium2 kernel written in Bass

```python
import jax, jax.numpy as jnp
from jax import lax
import numpy as np

D_MODEL = 1024
BATCH = 1
SEQ = 256
DEPTH = 2

N_MIXERS = 2
N_HEADS = 16
N_KV_HEADS = 4
HEAD_DIM = D_MODEL // N_HEADS
GROUP = N_HEADS // N_KV_HEADS
QKV_DIM = (N_HEADS + 2 * N_KV_HEADS) * HEAD_DIM
WINDOW = 128
BLOCK = 128
ROPE_THETA = 10000.0
CONV_WIDTH = 3
D_FF = 2816
N_SUBLAYERS = 3
N_ADA = 3 * N_SUBLAYERS
EPS = 1e-6
N_ATTN_LAYERS = (DEPTH + 1) // 2
N_CONV_LAYERS = DEPTH // 2

kernel_name = "hybrid_swa_sink_shortconv_macaron_adaln"

def rms_norm(x, gain):
    xf = x.astype(jnp.float32)
    y = xf * lax.rsqrt(jnp.mean(xf * xf, axis=-1, keepdims=True) + EPS)
    return (y * gain.astype(jnp.float32)).astype(x.dtype)

def modulate(h, shift, scale):
    return h * (1.0 + scale[:, None, :]) + shift[:, None, :]

def swiglu(h, w_up, w_down):
    gate, up = jnp.split(h @ w_up, 2, axis=-1)
    return (jax.nn.silu(gate) * up) @ w_down

def rope_tables(positions, dtype):
    inv_freq = ROPE_THETA ** (-jnp.arange(0, HEAD_DIM, 2, dtype=jnp.float32) / HEAD_DIM)
    ang = positions.astype(jnp.float32)[..., None] * inv_freq
    return jnp.cos(ang)[:, :, None, :].astype(dtype), jnp.sin(ang)[:, :, None, :].astype(dtype)

def apply_rope(t, cos, sin):
    t1, t2 = jnp.split(t, 2, axis=-1)
    return jnp.concatenate([t1 * cos - t2 * sin, t2 * cos + t1 * sin], axis=-1)

def swa_sink_attention(h, cos, sin, w_qkv, b_qkv, q_gain, k_gain, sinks, w_o, b_o):
    b, s, _ = h.shape
    nb = s // BLOCK
    qkv = h @ w_qkv + b_qkv
    q, k, v = jnp.split(qkv, [N_HEADS * HEAD_DIM, (N_HEADS + N_KV_HEADS) * HEAD_DIM], axis=-1)
    q = q.reshape(b, s, N_HEADS, HEAD_DIM)
    k = k.reshape(b, s, N_KV_HEADS, HEAD_DIM)
    v = v.reshape(b, s, N_KV_HEADS, HEAD_DIM)
    q = apply_rope(rms_norm(q, q_gain), cos, sin)
    k = apply_rope(rms_norm(k, k_gain), cos, sin)
    qb = q.reshape(b, nb, BLOCK, N_KV_HEADS, GROUP, HEAD_DIM)

    def banded(t):
        tb = t.reshape(b, nb, BLOCK, N_KV_HEADS, HEAD_DIM)
        prev = jnp.pad(tb[:, :-1], ((0, 0), (1, 0), (0, 0), (0, 0), (0, 0)))
        return jnp.concatenate([prev, tb], axis=2)

    kb, vb = banded(k), banded(v)
    scores = jnp.einsum('bnqkgd,bnskd->bnkgqs', qb, kb,
                        preferred_element_type=jnp.float32) * (HEAD_DIM ** -0.5)
    blk = jnp.arange(nb)[:, None, None] * BLOCK
    q_pos = blk + jnp.arange(BLOCK)[None, :, None]
    k_pos = blk - BLOCK + jnp.arange(2 * BLOCK)[None, None, :]
    rel = q_pos - k_pos
    mask = (rel >= 0) & (rel < WINDOW) & (k_pos >= 0)
    scores = jnp.where(mask[None, :, None, None], scores, -jnp.inf)
    sink = jnp.broadcast_to(sinks.astype(jnp.float32).reshape(1, 1, N_KV_HEADS, GROUP, 1, 1),
                            scores.shape[:-1] + (1,))
    probs = jax.nn.softmax(jnp.concatenate([scores, sink], axis=-1), axis=-1)[..., :-1]
    out = jnp.einsum('bnkgqs,bnskd->bnqkgd', probs.astype(vb.dtype), vb)
    return out.reshape(b, s, N_HEADS * HEAD_DIM) @ w_o + b_o

def short_gated_conv(h, w_in, conv_w, w_out):
    gb, gc, v = jnp.split(h @ w_in, 3, axis=-1)
    u = gc * v
    conv = lax.conv_general_dilated(
        u, conv_w[:, None, :], window_strides=(1,), padding=[(CONV_WIDTH - 1, 0)],
        dimension_numbers=('NWC', 'WIO', 'NWC'), feature_group_count=D_MODEL)
    return (gb * conv) @ w_out

def setup_inputs(seed: int = 0) -> dict:
    key = jax.random.key(seed)
    ks = jax.random.split(key, 20)
    f32 = jnp.float32
    d = D_MODEL
    nrm = lambda k, shape, fan_in: jax.random.normal(k, shape, f32) * (fan_in ** -0.5)
    x = jax.random.normal(ks[0], (BATCH, SEQ, d), f32)
    c = jax.random.normal(ks[1], (BATCH, d), f32)
    positions = (jnp.arange(SEQ, dtype=jnp.int32)[None, :]
                 + jax.random.randint(ks[2], (BATCH, 1), 0, 4096, dtype=jnp.int32))
    norm_gain = 1.0 + 0.05 * jax.random.normal(ks[3], (DEPTH, N_SUBLAYERS, d), f32)
    w_ada = nrm(ks[4], (DEPTH, d, N_ADA * d), d)
    b_ada = 0.02 * jax.random.normal(ks[5], (DEPTH, N_ADA * d), f32)
    w_ffn_up = nrm(ks[6], (DEPTH, 2, d, 2 * D_FF), d)
    w_ffn_down = nrm(ks[7], (DEPTH, 2, D_FF, d), D_FF)
    attn_w_qkv = nrm(ks[8], (N_ATTN_LAYERS, d, QKV_DIM), d)
    attn_b_qkv = 0.02 * jax.random.normal(ks[9], (N_ATTN_LAYERS, QKV_DIM), f32)
    attn_q_gain = 1.0 + 0.05 * jax.random.normal(ks[10], (N_ATTN_LAYERS, HEAD_DIM), f32)
    attn_k_gain = 1.0 + 0.05 * jax.random.normal(ks[11], (N_ATTN_LAYERS, HEAD_DIM), f32)
    attn_sinks = 0.5 * jax.random.normal(ks[12], (N_ATTN_LAYERS, N_HEADS), f32)
    attn_w_o = nrm(ks[13], (N_ATTN_LAYERS, N_HEADS * HEAD_DIM, d), N_HEADS * HEAD_DIM)
    attn_b_o = 0.02 * jax.random.normal(ks[14], (N_ATTN_LAYERS, d), f32)
    conv_w_in = nrm(ks[15], (N_CONV_LAYERS, d, 3 * d), d)
    conv_w = nrm(ks[16], (N_CONV_LAYERS, CONV_WIDTH, d), CONV_WIDTH)
    conv_w_out = nrm(ks[17], (N_CONV_LAYERS, d, d), d)
    return {"x": x, "c": c, "positions": positions, "norm_gain": norm_gain,
            "w_ada": w_ada, "b_ada": b_ada, "w_ffn_up": w_ffn_up, "w_ffn_down": w_ffn_down,
            "attn_w_qkv": attn_w_qkv, "attn_b_qkv": attn_b_qkv, "attn_q_gain": attn_q_gain,
            "attn_k_gain": attn_k_gain, "attn_sinks": attn_sinks, "attn_w_o": attn_w_o,
            "attn_b_o": attn_b_o, "conv_w_in": conv_w_in, "conv_w": conv_w,
            "conv_w_out": conv_w_out}

def reference(x, c, positions, norm_gain, w_ada, b_ada, w_ffn_up, w_ffn_down,
              attn_w_qkv, attn_b_qkv, attn_q_gain, attn_k_gain, attn_sinks, attn_w_o,
              attn_b_o, conv_w_in, conv_w, conv_w_out):
    cos, sin = rope_tables(positions, x.dtype)
    c_act = jax.nn.silu(c)
    for i in range(DEPTH):
        mod = c_act @ w_ada[i] + b_ada[i]
        sh1, sc1, g1, sh2, sc2, g2, sh3, sc3, g3 = jnp.split(mod, N_ADA, axis=-1)
        h = modulate(rms_norm(x, norm_gain[i, 0]), sh1, sc1)
        x = x + 0.5 * g1[:, None, :] * swiglu(h, w_ffn_up[i, 0], w_ffn_down[i, 0])
        h = modulate(rms_norm(x, norm_gain[i, 1]), sh2, sc2)
        j = i // N_MIXERS
        if i % N_MIXERS == 0:
            y = swa_sink_attention(h, cos, sin, attn_w_qkv[j], attn_b_qkv[j], attn_q_gain[j],
                                   attn_k_gain[j], attn_sinks[j], attn_w_o[j], attn_b_o[j])
        else:
            y = short_gated_conv(h, conv_w_in[j], conv_w[j], conv_w_out[j])
        x = x + g2[:, None, :] * y
        h = modulate(rms_norm(x, norm_gain[i, 2]), sh3, sc3)
        x = x + 0.5 * g3[:, None, :] * swiglu(h, w_ffn_up[i, 1], w_ffn_down[i, 1])
    return x


_drawn_inputs = setup_inputs


def setup_inputs(seed=0):
    import zlib

    import numpy as np

    out = dict(_drawn_inputs(seed))
    spreads = {}
    factors = {'attn_b_qkv': 3.461,
     'attn_q_gain': 7.375,
     'attn_k_gain': 8.0,
     'attn_sinks': 38.248,
     'attn_b_o': 3.785}
    for name, (base, spread) in spreads.items():
        noise = np.random.default_rng([zlib.crc32(name.encode()), seed]).standard_normal(out[name].shape)
        drawn = base * np.exp(spread * noise) if base else spread * noise
        out[name] = __import__('jax').numpy.asarray(drawn.astype(out[name].dtype))
    for name, factor in factors.items():
        out[name] = (out[name] * factor).astype(out[name].dtype)
    return out
```

```python
from contextlib import ExitStack
import math

import numpy as np

import concourse.bass as bass
from concourse import mybir
from concourse.alu_op_type import AluOpType as ALU

F32 = mybir.dt.float32
F32R = mybir.dt.float32r
I32 = mybir.dt.int32
ACT = mybir.ActivationFunctionType
AX = mybir.AxisListType

P = 128
D = 1024
T = 256
KC = D // P
FF = 2816
NF = FF // P
HEADS, KV, HD = 16, 4, 64
GROUP = HEADS // KV
HALF = HD // 2
EPS = 1e-6
N_ADA = 9
UP = 2 * KC * P
DN = D
AW = 512
AC = AW // P
KH = KC // 2
ADA_UNITS = 2 * N_ADA * D // AW
N_ADA_START = 2 * D // AW
MASKED = -3.0e38

FFN0, ATTN, FFN1, FFN2, CONV, FFN3 = range(6)
UPS = [NF, 6, NF, NF, 12, NF]
DOWNS = [NF, KC, NF, NF, KC, NF]
U0 = [sum(UPS[:n]) for n in range(6)]
D0 = [sum(DOWNS[:n]) for n in range(6)]
N_UP, N_DOWN = sum(UPS), sum(DOWNS)
FFN_NUMBER = {FFN0: 0, FFN1: 1, FFN2: 2, FFN3: 3}
ADA_OF = {FFN0: (N_ADA_START, NF // 2)}
ADA_ATTN = N_ADA_START + NF // 2
ADA_OF[FFN1] = (ADA_ATTN + 1, NF // 2)
ADA_OF[FFN2] = (ADA_ATTN + 1 + NF // 2, ADA_UNITS - (ADA_ATTN + 1 + NF // 2))
ADA_OF[FFN3] = (ADA_UNITS, 0)

COLS = {}
_at = 0
for _name, _n in (("c", KC), ("gain", 6 * KC), ("b_ada", 2 * N_ADA * KC), ("conv_w", 3 * KC), ("b_o", KC),
                  ("b_q", 2 * GROUP), ("b_k", 2), ("q_gain", 2), ("k_gain", 2), ("sinks", GROUP * 2 * KV),
                  ("inv_freq", 1), ("half_pi", 1), ("eps", 1)):
    COLS[_name] = (_at, _at + _n)
    _at += _n
N_COLS = _at
S_COLS = 3 * P


def build(nc, x_t, cols_d, pos_d, bv_d, ident_d, ones_d, heads_d, mask_d, w_ada, w_up, w_down, w_qkv, w_o,
          w_cin, w_cout, out_t):
    up_of = [w_up, w_qkv, w_up, w_up, w_cin, w_up]
    down_of = [w_down, w_o, w_down, w_down, w_cout, w_down]

    def first_row(ph):
        return FFN_NUMBER[ph] * NF if ph in FFN_NUMBER else 0

    with ExitStack() as ctx:
        def sb(name, shape, dt=F32):
            return ctx.enter_context(nc.sbuf_tensor(name, shape, dt))

        def sem(name):
            return ctx.enter_context(nc.semaphore(name))

        up_raw = sb("up_raw", [P, 2, UP])
        up_hi = sb("up_hi", [P, 2, UP], F32R)
        up_lo = sb("up_lo", [P, 2, UP], F32R)
        dn_raw = sb("dn_raw", [P, 2, DN])
        dn_hi = sb("dn_hi", [P, 2, DN], F32R)
        dn_lo = sb("dn_lo", [P, 2, DN], F32R)
        ada_raw = sb("ada_raw", [P, 2, KH * AW])
        ada_sum = sb("ada_sum", [P, AW])
        mod = sb("mod", [P, 2 * N_ADA * KC])
        cols = sb("cols", [P, N_COLS])
        c_act = sb("c_act", [P, KC])
        ident = sb("ident", [P, P])
        mean_w = sb("mean_w", [P, P])
        head_w = sb("head_w", [P, P])
        ones_c = sb("ones_c", [P, 1])
        mask = sb("mask", [P, S_COLS])
        pos = sb("pos", [P, T], I32)
        bv = sb("bv", [P, KV * HD])
        cos2 = sb("cos2", [P, 2 * T])
        sin2 = sb("sin2", [P, 2 * T])
        x = sb("x", [P, KC, T])
        sq = sb("sq", [P, KC, T])
        xs = sb("xs", [P, KC, T])
        h_hi = sb("h_hi", [P, KC, T], F32R)
        h_lo = sb("h_lo", [P, KC, T], F32R)
        ln_ms = sb("ln_ms", [P, T])
        rstd = sb("rstd", [P, T])
        table = sb("table", [P, 1])
        a_col = sb("a_col", [P, KC])
        g_col = sb("g_col", [P, KC])
        gb_col = sb("gb_col", [P, KC])
        gate_s = sb("gate_s", [P, 2, T])
        prod = sb("prod", [P, 2, T])
        a_hi = sb("a_hi", [P, 2, T], F32R)
        a_lo = sb("a_lo", [P, 2, T], F32R)
        qk_t = sb("qk_t", [P, 2 * T])
        qk_sq = sb("qk_sq", [P, 2 * T])
        qk_n = sb("qk_n", [P, 2 * T])
        qk_c = sb("qk_c", [P, 2 * T])
        qk_s = sb("qk_s", [P, 2 * T])
        ang = qk_c[:, :].rearrange("p (a t) -> p a t", a=2)
        qk_r = sb("qk_r", [P, T])
        k_rot = sb("k_rot", [P, 2 * T])
        q_rot = sb("q_rot", [P, 2, 2 * T])
        v_sb = sb("v_sb", [P, 2, KV * HD])
        probs = sb("probs", [P, 2, KV, S_COLS])
        m_col = sb("m_col", [P, 2, 2 * KV])
        nm_col = sb("nm_col", [P, 2, 2 * KV])
        sd_col = sb("sd_col", [P, 2, 2 * KV])
        es_col = sb("es_col", [P, 2, 2 * KV])
        su_col = sb("su_col", [P, 2, 2 * KV])
        de_col = sb("de_col", [P, 2, 2 * KV])
        ri_col = sb("ri_col", [P, 2, 2 * KV])
        p_t = sb("p_t", [P, 2, S_COLS])
        o_f = sq
        o_hi = sb("o_hi", [P, KC, T], F32R)
        o_lo = sb("o_lo", [P, KC, T], F32R)
        cv_u = sb("cv_u", [P, 2, 2 + T])
        cv_y = sb("cv_y", [P, 2, T])

        acc = [ctx.enter_context(nc.psum_tensor(f"acc{n}", [P, 2 * T], F32)) for n in range(4)]
        pair = [ctx.enter_context(nc.psum_tensor(f"pair{n}", [P, 2 * T], F32)) for n in range(2)]
        stat = ctx.enter_context(nc.psum_tensor("stat", [P, 2 * T], F32))
        aux = ctx.enter_context(nc.psum_tensor("aux", [P, 2 * T], F32))

        consts_in = sem("consts_in")
        x_in = sem("x_in")
        up_in = [sem(f"up_in{n}") for n in range(2)]
        dn_in = [sem(f"dn_in{n}") for n in range(2)]
        ada_in = [sem(f"ada_in{n}") for n in range(2)]
        cols_in, pos_in, mean_w_in = sem("cols_in"), sem("pos_in"), sem("mean_w_in")
        start_in = [sem(f"start_in{n}") for n in range(2)]
        stored = sem("stored")
        up_hi_done, up_lo_done = sem("up_hi_done"), sem("up_lo_done")
        dn_hi_done, dn_lo_done = sem("dn_hi_done"), sem("dn_lo_done")
        up_done, dn_done = sem("up_done"), sem("dn_done")
        bank_done = sem("bank_done")
        c_done = sem("c_done")
        ada_step = sem("ada_step")
        ada_red = sem("ada_red")
        ada_fin = sem("ada_fin")
        x_done, sq_done, mean_done, rstd_done = sem("x_done"), sem("sq_done"), sem("mean_done"), sem("rstd_done")
        ln_done, xs_done, hh_done, h_done = sem("ln_done"), sem("xs_done"), sem("hh_done"), sem("h_done")
        col_step = sem("col_step")
        gate_done, prod_done, ah_done, al_done = sem("gate_done"), sem("prod_done"), sem("ah_done"), sem("al_done")
        tab_step, tab_done = sem("tab_step"), sem("tab_done")
        biased, squared, head_mean, head_rstd, rope_step, rot_done = (sem(n) for n in (
            "biased", "squared", "head_mean", "head_rstd", "rope_step", "rot_done"))
        v_done, scored, masked, soft_step, exp_done, norm_done = (sem(n) for n in (
            "v_done", "scored", "masked", "soft_step", "exp_done", "norm_done"))
        shift_done, pt_ready, pt_done, pv_done, of_done, oh_done, ol_done = (sem(n) for n in (
            "shift_done", "pt_ready", "pt_done", "pv_done", "of_done", "oh_done", "ol_done"))
        cv_c, cv_in, cv_step, cv_pad = sem("cv_c"), sem("cv_in"), sem("cv_step"), sem("cv_pad")

        def col(name, a=0, n=None):
            lo, hi = COLS[name]
            return cols[:, lo + a:hi if n is None else lo + a + n]

        def mod_cols(layer, v):
            at = (layer * N_ADA + v) * KC
            return mod[:, at:at + KC]

        N_CONST_DMAS = 4
        start_slots = [(ada_raw[:, 0, :], ada_in[0]), (ada_raw[:, 1, :], ada_in[1]),
                       (xs[:, :, :].rearrange("p k t -> p (k t)"), start_in[0]),
                       (probs[:, :, :, :].rearrange("p a g n -> p (a g n)")[:, 0:KH * AW], start_in[1])]
        norm_of = {FFN0: (0, 0), ATTN: (0, 1), FFN1: (0, 2), FFN2: (1, 0), CONV: (1, 1), FFN3: (1, 2)}

        block = ctx.enter_context(nc.Block())

        def ada_total(n):
            return qk_n[:, :] if isinstance(n, int) and n < N_ADA_START and n % 2 else ada_sum[:, :]

        def ada_bank(n):
            return acc[n] if isinstance(n, int) and n < N_ADA_START else aux

        @block.sync
        def _(sp):
            def load_up(ph, f, s):
                n = U0[ph] + f
                if not isinstance(n, int) or n >= 2:
                    sp.wait_ge(up_lo_done, n - 1)
                sp.dma_start(up_raw[:, s, :],
                             up_of[ph][bass.ds(first_row(ph) + f, 1), :, :].rearrange("a p n -> p (a n)")
                             ).then_inc(up_in[s], 16)

            def load_down(ph, f, s):
                n = D0[ph] + f
                if not isinstance(n, int) or n >= 2:
                    sp.wait_ge(dn_lo_done, n - 1)
                sp.dma_start(dn_raw[:, s, :],
                             down_of[ph][bass.ds(first_row(ph) + f, 1), :, :].rearrange("a p n -> p (a n)")
                             ).then_inc(dn_in[s], 16)

            def load_start(h):
                slot, landed = start_slots[h % 4]
                if h >= 4:
                    sp.wait_ge(ada_step, KH * (h - 3))
                sp.dma_start(slot, w_ada[h, :, :]).then_inc(landed, 16)

            sp.dma_start(cols[:, :], cols_d).then_inc(cols_in, 16)
            sp.dma_start(pos[:, :], pos_d.partition_broadcast(P)).then_inc(pos_in, 16)
            for h in range(4):
                load_start(h)
            sp.dma_start(x[:, :, :], x_t.rearrange("(k p) t -> p k t", p=P)).then_inc(x_in, 16)
            sp.dma_start(mean_w[:, :], ones_d).then_inc(mean_w_in, 16)
            for h in (4, 5, 7, 6):
                load_start(h)
            load_up(FFN0, 0, 0)
            load_up(FFN0, 1, 1)
            load_down(FFN0, 0, 0)
            sp.dma_start(bv[:, :], bv_d.partition_broadcast(P)).then_inc(consts_in, 16)
            sp.dma_start(ident[:, :], ident_d).then_inc(consts_in, 16)
            sp.dma_start(head_w[:, :], heads_d).then_inc(consts_in, 16)
            sp.dma_start(mask[:, :], mask_d).then_inc(consts_in, 16)

            def ffn_loads(ph, ups_there=False):
                if not ups_there:
                    load_up(ph, 0, 0)
                    load_up(ph, 1, 1)
                if ph != FFN0:
                    load_down(ph, 0, 0)
                with sp.Fori(1, NF // 2) as i:
                    load_up(ph, 2 * i, 0)
                    load_down(ph, 2 * i - 1, 1)
                    load_up(ph, 2 * i + 1, 1)
                    load_down(ph, 2 * i, 0)
                load_down(ph, NF - 1, 1)

            ffn_loads(FFN0, ups_there=True)
            for kind, n in (("u", 0), ("d", 0), ("u", 1), ("u", 2), ("d", 1), ("u", 3), ("d", 2), ("u", 4),
                            ("u", 5), ("d", 3), ("next", 0), ("next", 1), ("d", 4), ("d", 5), ("d", 6), ("d", 7)):
                if kind == "next":
                    load_up(FFN1, n, n)
                else:
                    (load_up if kind == "u" else load_down)(ATTN, n, n % 2)
            ffn_loads(FFN1, ups_there=True)
            ffn_loads(FFN2)
            for i in range(4):
                load_up(CONV, 3 * i, (3 * i) % 2)
                if i:
                    load_down(CONV, 2 * i - 1, 1)
                load_up(CONV, 3 * i + 1, (3 * i + 1) % 2)
                load_up(CONV, 3 * i + 2, (3 * i + 2) % 2)
                load_down(CONV, 2 * i, 0)
            load_down(CONV, KC - 1, 1)
            ffn_loads(FFN3)
            for j in range(KC):
                sp.wait_ge(x_done, 6 * KC + j + 1 - KC)
                sp.dma_start(out_t[j * P:(j + 1) * P, :], x[:, j, :]).then_inc(stored, 16)
            sp.wait_ge(stored, 16 * KC)

        @block.scalar
        def _(act):
            def round_up(n, s):
                if isinstance(n, int) and n >= N_UP:
                    return
                act.wait_ge(up_in[s], 8 * (n - s) + 16)
                if not isinstance(n, int) or n >= 2:
                    act.wait_ge(up_done, n - 1)
                nc.scalar.activation(up_hi[:, s, :], up_raw[:, s, :], ACT.Copy).then_inc(up_hi_done, 1)

            def round_down(n, s):
                if isinstance(n, int) and n >= N_DOWN:
                    return
                act.wait_ge(dn_in[s], 8 * (n - s) + 16)
                if not isinstance(n, int) or n >= 2:
                    act.wait_ge(dn_done, n - 1)
                nc.scalar.activation(dn_hi[:, s, :], dn_raw[:, s, :], ACT.Copy).then_inc(dn_hi_done, 1)

            def load_table(function):
                nc.scalar.activation(table[:, :], col("eps"), function)

            def load_half(n, s):
                if isinstance(n, int) and n >= ADA_UNITS:
                    return
                if isinstance(n, int) and n == N_ADA_START:
                    act.wait_ge(ada_step, KH * (5 + s))
                else:
                    act.wait_ge(ada_step, 8 * n + 4 * s - 4)
                act.dma_start(ada_raw[:, s, :],
                              w_ada[bass.ds(2 * n + s, 1), :, :].rearrange("a p n -> p (a n)")
                              ).then_inc(ada_in[s], 16)

            def squares(ph):
                load_table(ACT.Ln)
                for j in range(KC):
                    if ph == FFN0:
                        if j == 0:
                            act.wait_ge(x_in, 16)
                    else:
                        act.wait_ge(x_done, (ph - 1) * KC + j + 1)
                    nc.scalar.activation(sq[:, j, :], x[:, j, :], ACT.Square).then_inc(sq_done, 1)

            def scale(ph):
                act.wait_ge(mean_done, ph + 1)
                nc.scalar.activation(ln_ms[:, :], stat[:, 0:T], ACT.Ln, bias=col("eps")).then_inc(ln_done, 1)
                act.wait_ge(ln_done, ph + 1)
                nc.scalar.activation(rstd[:, :], ln_ms[:, :], ACT.Exp, scale=-0.5).then_inc(rstd_done, 1)

            def shifted(ph):
                layer, sub = norm_of[ph]
                shift = mod_cols(layer, 3 * sub)
                for j in range(KC):
                    act.wait_ge(xs_done, ph * KC + j + 1)
                    nc.scalar.activation(h_hi[:, j, :], xs[:, j, :], ACT.Identity,
                                         bias=shift[:, j:j + 1]).then_inc(hh_done, 1)
                if ph in FFN_NUMBER:
                    load_table(ACT.Silu)

            def norm(ph):
                squares(ph)
                scale(ph)
                shifted(ph)

            def hidden(ph, f, s):
                g = FFN_NUMBER[ph] * NF + f
                act.wait_ge(up_done, U0[ph] + f + 1)
                nc.scalar.activation(gate_s[:, s, :], pair[s][:, 0:T], ACT.Silu).then_inc(gate_done, 1)
                if not isinstance(f, int) or f >= 2:
                    act.wait_ge(dn_done, D0[ph] + f - 1)
                act.wait_ge(prod_done, g + 1)
                nc.scalar.activation(a_hi[:, s, :], prod[:, s, :], ACT.Copy).then_inc(ah_done, 1)

            def ffn(ph):
                first, count = ADA_OF[ph]

                def period(f, s, n):
                    hidden(ph, f, s)
                    round_up(U0[ph] + f + 2, s)
                    round_down(D0[ph] + f + 1, 1 - s)
                    if n is not None:
                        load_half(n + 1, s)
                last = NF // 2 - 1
                if ph != FFN0:
                    norm(ph)
                if ph == FFN2:
                    round_down(D0[ph], 0)
                    load_half(first, 1)
                stop = min(last, count - 1) if count else last
                period(0, 0, first if count else None)
                period(1, 1, first if count else None)
                with act.Fori(1, stop) as i:
                    period(2 * i, 0, first + i if count else None)
                    period(2 * i + 1, 1, first + i if count else None)
                for i in range(stop, last):
                    period(2 * i, 0, first + i if i < count else None)
                    period(2 * i + 1, 1, first + i if i < count else None)
                period(NF - 2, 0, first + last if count > last else None)
                hidden(ph, NF - 1, 1)
                round_up(U0[ph] + NF + 1, 1)

            act.wait_ge(cols_in, 16)
            nc.scalar.activation(c_act[:, :], col("c"), ACT.Silu).then_inc(c_done, 1)
            act.wait_ge(tab_step, 8)
            for t in range(2):
                nc.scalar.activation(sin2[:, t * T:(t + 1) * T], ang[:, 0, :], ACT.Sin).then_inc(tab_done, 1)
                nc.scalar.activation(cos2[:, t * T:(t + 1) * T], ang[:, 1, :], ACT.Sin, scale=-1.0,
                                     bias=col("half_pi")).then_inc(tab_done, 1)
            squares(FFN0)
            scale(FFN0)
            load_half(N_ADA_START, 0)
            load_half(N_ADA_START, 1)
            round_up(0, 0)
            shifted(FFN0)
            round_up(1, 1)
            round_down(0, 0)
            ffn(FFN0)

            def bias_square(n, b):
                act.wait_ge(up_done, U0[ATTN] + (1 if n == 0 else n + 2))
                if n >= 1:
                    act.wait_ge(rope_step, 5 * n)
                for t in range(2):
                    ins = nc.scalar.activation(qk_t[:, t * T:(t + 1) * T], pair[(0 if n == 0 else n + 1) % 2][:, t * T:(t + 1) * T],
                                               ACT.Identity, bias=b[:, t:t + 1]).then_inc(biased, 1)
                act.wait_ge(biased, 2 * n + 2)
                nc.scalar.activation(qk_sq[:, :], qk_t[:, :], ACT.Square).then_inc(squared, 1)

            def head_scale(n):
                act.wait_ge(head_mean, n + 1)
                nc.scalar.activation(qk_r[:, :], stat[:, 0:T], ACT.Ln, bias=col("eps")).then_inc(head_rstd, 1)
                act.wait_ge(head_rstd, 2 * n + 1)
                nc.scalar.activation(qk_r[:, :], qk_r[:, :], ACT.Exp, scale=-0.5).then_inc(head_rstd, 1)

            def exps(r):
                act.wait_ge(soft_step, 5 * r + 5)
                s = r % 2
                for b in range(2):
                    for g in range(KV):
                        e = probs[:, s, g, 0:P] if b == 0 else probs[:, s, g, P:S_COLS]
                        nc.scalar.activation(e, e, ACT.Exp, bias=nm_col[:, s, b * KV + g:b * KV + g + 1],
                                             accum_out=su_col[:, s, b * KV + g:b * KV + g + 1]).then_inc(exp_done, 1)
                nc.scalar.activation(es_col[:, s, :], sd_col[:, s, :], ACT.Exp).then_inc(exp_done, 1)

            def outputs(r):
                for g in range(KV):
                    n = KV * r + g
                    act.wait_ge(pt_ready, n + 1)
                    if n >= 2:
                        act.wait_ge(pv_done, n - 1)
                    nc.scalar.activation(p_t[:, g % 2, :], acc[2 + g % 2][:, 0:S_COLS], ACT.Copy).then_inc(pt_done, 1)
                    if g % 2:
                        t = 2 * r + g // 2
                        act.wait_ge(pv_done, n + 1)
                        nc.scalar.activation(o_f[:, t, :], aux[:, 0:T], ACT.Copy).then_inc(of_done, 1)
                        act.wait_ge(of_done, t + 1)
                        nc.scalar.activation(o_hi[:, t, :], o_f[:, t, :], ACT.Copy).then_inc(oh_done, 1)

            norm(ATTN)
            round_down(D0[ATTN], 0)
            load_half(ADA_ATTN, 1)
            bias_square(0, col("b_k"))
            round_up(U0[ATTN] + 2, 0)
            round_up(U0[ATTN] + 3, 1)
            head_scale(0)
            round_down(D0[ATTN] + 1, 1)
            bias_square(1, col("b_q", 0, 2))
            round_up(U0[ATTN] + 4, 0)
            head_scale(1)
            load_half(ADA_ATTN + 1, 0)
            load_half(ADA_ATTN + 1, 1)
            for r in range(GROUP):
                if r < GROUP - 1:
                    bias_square(r + 2, col("b_q", 2 * r + 2, 2))
                    round_up(U0[ATTN] + r + 5, (r + 5) % 2)
                    head_scale(r + 2)
                if r:
                    outputs(r - 1)
                exps(r)
            outputs(GROUP - 1)
            for t in range(KC - 1):
                round_down(D0[ATTN] + t + 2, t % 2)

            ffn(FFN1)
            ffn(FFN2)

            norm(CONV)
            round_down(D0[CONV], 0)
            for i in range(KC // 2):
                for s in range(2):
                    u = 3 * i + s
                    act.wait_ge(up_done, U0[CONV] + u + 1)
                    nc.scalar.activation(gate_s[:, s, :], pair[u % 2][:, 0:T], ACT.Copy).then_inc(cv_c, 1)
                    round_up(U0[CONV] + u + 2, u % 2)
                    if s == 0 and i:
                        round_down(D0[CONV] + 2 * i - 1, 1)
                for s in range(2):
                    act.wait_ge(cv_step, 10 * i + 2 * s + 8)
                    if s == 0 and i:
                        act.wait_ge(dn_done, D0[CONV] + 2 * i)
                    nc.scalar.activation(a_hi[:, s, :], cv_y[:, s, :], ACT.Copy).then_inc(ah_done, 1)
                round_up(U0[CONV] + 3 * i + 4, (3 * i + 4) % 2)
                if i:
                    round_down(D0[CONV] + 2 * i, 0)
            round_down(D0[CONV] + KC - 1, 1)
            round_down(D0[CONV] + KC, 0)
            ffn(FFN3)

        @block.vector
        def _(dve):
            def rest_up(n, s):
                if isinstance(n, int) and n >= N_UP:
                    return
                dve.wait_ge(up_hi_done, n + 1)
                nc.vector.tensor_tensor(up_lo[:, s, :], up_raw[:, s, :], up_hi[:, s, :].bitcast(F32),
                                        ALU.subtract).then_inc(up_lo_done, 1)

            def rest_down(n, s):
                if isinstance(n, int) and n >= N_DOWN:
                    return
                dve.wait_ge(dn_hi_done, n + 1)
                nc.vector.tensor_tensor(dn_lo[:, s, :], dn_raw[:, s, :], dn_hi[:, s, :].bitcast(F32),
                                        ALU.subtract).then_inc(dn_lo_done, 1)

            def keep_mod(n):
                dve.wait_ge(ada_red, n + 1)
                nc.vector.tensor_tensor(mod[:, bass.ds(AC * n, AC)], ada_bank(n)[:, 0:AC],
                                        cols[:, bass.ds(COLS["b_ada"][0] + AC * n, AC)],
                                        ALU.add).then_inc(ada_fin, 1)

            def ada_half(n, s, keep=True):
                if s == 0 and keep:
                    keep_mod(n - 1)
                if isinstance(n, int) and n < N_ADA_START:
                    slot, landed = start_slots[(2 * n + s) % 4]
                    dve.wait_ge(landed, 16 * (n // 2 + 1))
                else:
                    slot = ada_raw[:, s, :]
                    dve.wait_ge(ada_in[s], 16 * (n - 1))
                total = ada_total(n)
                for k in range(KH):
                    w = slot[:, k * AW:(k + 1) * AW]
                    c = c_act[:, s * KH + k:s * KH + k + 1]
                    if s == 0 and k == 0:
                        nc.vector.tensor_scalar(total, w, c, None, ALU.mult).then_inc(ada_step, 1)
                    else:
                        dve.wait_ge(ada_step, 8 * n + 4 * s + k)
                        ends = isinstance(n, int) and n == N_ADA_START - 1 and k == KH - 1
                        nc.vector.scalar_tensor_tensor(out=total, in0=w, scalar=c, in1=total,
                                                       op0=ALU.mult, op1=ALU.add).then_inc(ada_step, 1 + KH * ends)

            small = [0]

            def column(ins):
                ins.then_inc(col_step, 1)
                small[0] += 1
                dve.wait_ge(col_step, small[0])

            def prepare(ph, units):
                layer, sub = norm_of[ph]
                dve.wait_ge(ada_fin, units)
                column(nc.vector.scalar_tensor_tensor(
                    out=a_col[:, :], in0=mod_cols(layer, 3 * sub + 1), scalar=1.0,
                    in1=col("gain", (3 * layer + sub) * KC, KC), op0=ALU.add, op1=ALU.mult))

            def add_output(ph):
                layer, sub = norm_of[ph]
                column(nc.vector.tensor_scalar(g_col[:, :], mod_cols(layer, 3 * sub + 2),
                                               0.5 if ph in FFN_NUMBER else 1.0, None, ALU.mult))
                for j in range(KC):
                    if j % 2 == 0 and j < KC - 2:
                        dve.wait_ge(bank_done, 3 * ph + j // 2 + 1)
                    elif j == KC - 2:
                        dve.wait_ge(dn_done, D0[ph] + DOWNS[ph])
                    nc.vector.scalar_tensor_tensor(out=x[:, j, :], in0=acc[j // 2][:, (j % 2) * T:(j % 2 + 1) * T],
                                                   scalar=g_col[:, j:j + 1], in1=x[:, j, :],
                                                   op0=ALU.mult, op1=ALU.add).then_inc(x_done, 1)

            def norm(ph):
                dve.wait_ge(rstd_done, ph + 1)
                layer, sub = norm_of[ph]
                shift = mod_cols(layer, 3 * sub)

                def rest(j):
                    dve.wait_ge(hh_done, ph * KC + j + 1)
                    nc.vector.scalar_tensor_tensor(out=h_lo[:, j, :], in0=xs[:, j, :], scalar=shift[:, j:j + 1],
                                                   in1=h_hi[:, j, :].bitcast(F32), op0=ALU.add,
                                                   op1=ALU.subtract).then_inc(h_done, 1)
                for j in range(KC):
                    nc.vector.scalar_tensor_tensor(out=xs[:, j, :], in0=x[:, j, :], scalar=a_col[:, j:j + 1],
                                                   in1=rstd[:, :], op0=ALU.mult, op1=ALU.mult).then_inc(xs_done, 1)
                    if j >= 2:
                        rest(j - 2)
                rest(KC - 2)
                rest(KC - 1)

            def hidden(ph, f, s):
                g = FFN_NUMBER[ph] * NF + f
                dve.wait_ge(gate_done, g + 1)
                nc.vector.tensor_tensor(prod[:, s, :], gate_s[:, s, :], pair[s][:, T:2 * T], ALU.mult).then_inc(prod_done, 1)
                dve.wait_ge(ah_done, AH0[ph] + f + 1)
                nc.vector.tensor_tensor(a_lo[:, s, :], prod[:, s, :], a_hi[:, s, :].bitcast(F32),
                                        ALU.subtract).then_inc(al_done, 1)

            def ffn(ph, rest_first):
                first, count = ADA_OF[ph]
                if ph != FFN0:
                    norm(ph)
                if rest_first:
                    rest_down(D0[ph], 0)
                if PENDING_HALF[ph] is not None:
                    ada_half(PENDING_HALF[ph], 1)

                def period(f, s, n, keep=True):
                    hidden(ph, f, s)
                    if n is not None:
                        ada_half(n, s, keep)
                    rest_up(U0[ph] + f + 2, s)
                    rest_down(D0[ph] + f + 1, 1 - s)

                last = NF // 2 - 1
                period(0, 0, first if count else None, KEEP_FIRST[ph])
                period(1, 1, first if count else None)
                with dve.Fori(1, min(last, count) if count else last) as i:
                    period(2 * i, 0, first + i if count else None)
                    period(2 * i + 1, 1, first + i if count else None)
                if count and count < last:
                    period(2 * count, 0, None)
                    keep_mod(first + count - 1)
                    period(2 * count + 1, 1, None)
                    for f in range(2 * count + 2, 2 * last):
                        period(f, f % 2, None)
                period(NF - 2, 0, first + last if count > last else None)
                hidden(ph, NF - 1, 1)
                add_output(ph)
                rest_up(U0[ph] + NF + 1, 1)

            PENDING_HALF = {ph: None for ph in ADA_OF}
            PENDING_HALF[FFN2] = ADA_OF[FFN1][0] + NF // 2 - 1
            KEEP_FIRST = {FFN0: False, FFN1: False, FFN2: True, FFN3: False}

            nc.vector.memset(ones_c[:, :], 1.0).then_inc(cv_pad, 1)
            nc.vector.memset(cv_u[:, :, 0:2], 0.0).then_inc(cv_pad, 1)
            dve.wait_ge(cols_in, 16)
            dve.wait_ge(pos_in, 16)
            two_pi = 2 * math.pi
            part1 = 6.28125
            part2 = float(np.float32(round((two_pi - part1) * 2 ** 19) / 2 ** 19))
            part3 = float(np.float32(two_pi - part1 - part2))
            magic = 1.5 * 2 ** 23
            steps = [0]

            def angle(ins):
                ins.then_inc(tab_step, 1)
                steps[0] += 1
                dve.wait_ge(tab_step, steps[0])
            angle(nc.vector.tensor_scalar(ang[:, 0, :], pos[:, :], col("inv_freq"), None, ALU.mult))
            angle(nc.vector.tensor_scalar(ang[:, 1, :], ang[:, 0, :], 1 / two_pi, magic, ALU.mult, ALU.add))
            angle(nc.vector.tensor_scalar(ang[:, 1, :], ang[:, 1, :], magic, None, ALU.subtract))
            for part in (part1, part2, part3):
                angle(nc.vector.scalar_tensor_tensor(out=ang[:, 0, :], in0=ang[:, 1, :], scalar=-part, in1=ang[:, 0, :],
                                                     op0=ALU.mult, op1=ALU.add))
            pi = float(np.nextafter(np.float32(math.pi), np.float32(0)))
            angle(nc.vector.tensor_scalar(ang[:, 0, :], ang[:, 0, :], pi, -pi, ALU.min, ALU.max))
            angle(nc.vector.scalar_tensor_tensor(out=ang[:, 1, :], in0=ang[:, 0, :], scalar=-1.0, in1=ang[:, 0, :],
                                                 op0=ALU.mult, op1=ALU.max))

            dve.wait_ge(c_done, 1)
            for n in range(N_ADA_START):
                if n >= 2:
                    dve.wait_ge(ada_red, n - 1)
                ada_half(n, 0, keep=False)
                if n < N_ADA_START - 1:
                    ada_half(n, 1)
            rest_up(0, 0)
            for n in range(N_ADA_START):
                keep_mod(n)
            prepare(FFN0, N_ADA_START)
            norm(FFN0)
            rest_up(1, 1)
            rest_down(0, 0)
            ffn(FFN0, False)

            rope = [0]

            def rotate(n, gain, dst):
                def step(ins):
                    ins.then_inc(rope_step, 1)
                    rope[0] += 1
                dve.wait_ge(head_rstd, 2 * n + 2)
                for t in range(2):
                    step(nc.vector.scalar_tensor_tensor(out=qk_n[:, t * T:(t + 1) * T], in0=qk_t[:, t * T:(t + 1) * T],
                                                        scalar=gain[:, t:t + 1], in1=qk_r[:, :],
                                                        op0=ALU.mult, op1=ALU.mult))
                dve.wait_ge(rope_step, rope[0])
                step(nc.vector.tensor_tensor(qk_c[:, :], qk_n[:, :], cos2[:, :], ALU.mult))
                step(nc.vector.tensor_tensor(qk_s[:, :], qk_n[:, :], sin2[:, :], ALU.mult))
                dve.wait_ge(rope_step, rope[0])
                step(nc.vector.tensor_tensor(dst[:, 0:T], qk_c[:, 0:T], qk_s[:, T:2 * T], ALU.subtract))
                nc.vector.tensor_tensor(dst[:, T:2 * T], qk_c[:, T:2 * T], qk_s[:, 0:T], ALU.add).then_inc(rot_done, 1)

            def softmax_columns(r):
                s = r % 2
                for g in range(KV):
                    dve.wait_ge(scored, KV * r + g + 1)
                    nc.vector.scalar_tensor_tensor(out=probs[:, s, g, :], in0=acc[g % 2][:, 0:S_COLS], scalar=HD ** -0.5,
                                                   in1=mask[:, :], op0=ALU.mult, op1=ALU.add).then_inc(masked, 1)
                dve.wait_ge(masked, KV * r + KV)
                nc.vector.tensor_reduce(m_col[:, s, 0:KV], probs[:, s, :, 0:P], AX.X, ALU.max).then_inc(soft_step, 1)
                nc.vector.tensor_reduce(m_col[:, s, KV:2 * KV], probs[:, s, :, P:S_COLS], AX.X, ALU.max).then_inc(soft_step, 1)
                dve.wait_ge(soft_step, 5 * r + 2)
                sink = col("sinks", r * 2 * KV, 2 * KV)
                nc.vector.tensor_tensor(m_col[:, s, :], m_col[:, s, :], sink, ALU.max).then_inc(soft_step, 1)
                dve.wait_ge(soft_step, 5 * r + 3)
                nc.vector.tensor_scalar(nm_col[:, s, :], m_col[:, s, :], -1.0, None, ALU.mult).then_inc(soft_step, 1)
                nc.vector.tensor_tensor(sd_col[:, s, :], sink, m_col[:, s, :], ALU.subtract).then_inc(soft_step, 1)

            def normalise(r):
                s = r % 2
                dve.wait_ge(exp_done, 9 * r + 9)
                column(nc.vector.tensor_tensor(de_col[:, s, :], su_col[:, s, :], es_col[:, s, :], ALU.add))
                column(nc.vector.reciprocal(ri_col[:, s, :], de_col[:, s, :]))
                for g in range(KV):
                    for b in range(2):
                        e = probs[:, s, g, 0:P] if b == 0 else probs[:, s, g, P:S_COLS]
                        nc.vector.tensor_scalar(e, e, ri_col[:, s, b * KV + g:b * KV + g + 1], None,
                                                ALU.mult).then_inc(norm_done, 1)

            def rest_outputs(r):
                for t in (2 * r, 2 * r + 1):
                    dve.wait_ge(oh_done, t + 1)
                    nc.vector.tensor_tensor(o_lo[:, t, :], o_f[:, t, :], o_hi[:, t, :].bitcast(F32),
                                            ALU.subtract).then_inc(ol_done, 1)

            prepare(ATTN, N_ADA_START + 6)
            norm(ATTN)
            dve.wait_ge(consts_in, 16 * N_CONST_DMAS)
            rest_down(D0[ATTN], 0)
            ada_half(ADA_ATTN - 1, 1)
            rest_up(U0[ATTN] + 2, 0)
            dve.wait_ge(up_done, U0[ATTN] + 2)
            for b in range(2):
                nc.vector.tensor_tensor(v_sb[:, b, :], pair[1][:, b * T:(b + 1) * T], bv[:, :], ALU.add).then_inc(v_done, 1)
            rest_up(U0[ATTN] + 3, 1)
            rotate(0, col("k_gain"), k_rot)
            rest_down(D0[ATTN] + 1, 1)
            ada_half(ADA_ATTN, 0)
            rest_up(U0[ATTN] + 4, 0)
            rotate(1, col("q_gain"), q_rot[:, 0, :])
            ada_half(ADA_ATTN, 1)
            for r in range(GROUP):
                softmax_columns(r)
                if r < GROUP - 1:
                    rest_up(U0[ATTN] + r + 5, (r + 5) % 2)
                    rotate(r + 2, col("q_gain"), q_rot[:, (r + 1) % 2, :])
                if r:
                    rest_outputs(r - 1)
                normalise(r)
                if r == 0:
                    keep_mod(ADA_ATTN)
            column(nc.vector.tensor_tensor(gb_col[:, :], mod_cols(0, 5), col("b_o"), ALU.mult))
            for j in range(KC):
                column(nc.vector.tensor_scalar(x[:, j, :], x[:, j, :], gb_col[:, j:j + 1], None, ALU.add))
            rest_outputs(GROUP - 1)
            for t in range(KC - 1):
                rest_down(D0[ATTN] + t + 2, t % 2)
            add_output(ATTN)

            prepare(FFN1, ADA_ATTN + 1)
            ffn(FFN1, False)
            prepare(FFN2, N_ADA_START + 18)
            ffn(FFN2, True)

            prepare(CONV, ADA_UNITS)
            norm(CONV)
            rest_down(D0[CONV], 0)
            for i in range(KC // 2):
                def conv(s):
                    j = 2 * i + s
                    u = cv_u[:, s, :]
                    dve.wait_ge(cv_c, j + 1)
                    n = 10 * i + 5 * s
                    nc.vector.tensor_tensor(u[:, 2:2 + T], gate_s[:, s, :], pair[(3 * i + s) % 2][:, T:2 * T],
                                            ALU.mult).then_inc(cv_in, 1)
                    dve.wait_ge(cv_in, j + 1)
                    for w in range(3):
                        tap = col("conv_w", w * KC + j, 1)
                        if w == 0:
                            nc.vector.tensor_scalar(prod[:, s, :], u[:, 0:T], tap, None, ALU.mult).then_inc(cv_step, 1)
                        else:
                            dve.wait_ge(cv_step, n0[0])
                            nc.vector.scalar_tensor_tensor(out=prod[:, s, :], in0=u[:, w:w + T], scalar=tap,
                                                           in1=prod[:, s, :], op0=ALU.mult, op1=ALU.add).then_inc(cv_step, 1)
                        n0[0] += 1
                n0 = [10 * i]
                conv(0)
                rest_up(U0[CONV] + 3 * i + 2, (3 * i + 2) % 2)
                if i:
                    rest_down(D0[CONV] + 2 * i - 1, 1)
                conv(1)
                rest_up(U0[CONV] + 3 * i + 3, (3 * i + 3) % 2)
                dve.wait_ge(up_done, U0[CONV] + 3 * i + 3)
                dve.wait_ge(cv_step, n0[0])
                for s in range(2):
                    nc.vector.tensor_tensor(cv_y[:, s, :], prod[:, s, :], pair[(3 * i + 2) % 2][:, s * T:(s + 1) * T],
                                            ALU.mult).then_inc(cv_step, 2)
                    n0[0] += 2
                for s in range(2):
                    dve.wait_ge(ah_done, AH0[CONV] + 2 * i + s + 1)
                    nc.vector.tensor_tensor(a_lo[:, s, :], cv_y[:, s, :], a_hi[:, s, :].bitcast(F32),
                                            ALU.subtract).then_inc(al_done, 1)
                rest_up(U0[CONV] + 3 * i + 4, (3 * i + 4) % 2)
                if i:
                    rest_down(D0[CONV] + 2 * i, 0)
            rest_down(D0[CONV] + KC - 1, 1)
            rest_down(D0[CONV] + KC, 0)
            add_output(CONV)
            prepare(FFN3, ADA_UNITS)
            ffn(FFN3, False)

        @block.tensor
        def _(pe):
            def three(out, w_hi, w_lo, m_hi, m_lo, start, stop):
                nc.tensor.matmul(out, w_hi, m_hi, start=start, stop=False, skip_group_check=True)
                nc.tensor.matmul(out, w_hi, m_lo, start=False, stop=False, skip_group_check=True)
                return nc.tensor.matmul(out, w_lo, m_hi, start=False, stop=stop, skip_group_check=True)

            def up(ph, f, s, first=False):
                pe.wait_ge(up_lo_done, U0[ph] + f + 1)
                for k in range(KC):
                    if first:
                        pe.wait_ge(h_done, ph * KC + k + 1)
                    for c in range(2):
                        at = (2 * k + c) * P
                        ins = three(pair[s][:, c * T:(c + 1) * T], up_hi[:, s, at:at + P], up_lo[:, s, at:at + P],
                                    h_hi[:, k, :], h_lo[:, k, :], k == 0 and c == 0, k == KC - 1)
                ins.then_inc(up_done, 1)

            def down(n, s, m_hi, m_lo, first=False, last=False):
                pe.wait_ge(dn_lo_done, n + 1)
                for j in range(KC):
                    ins = three(acc[j // 2][:, (j % 2) * T:(j % 2 + 1) * T], dn_hi[:, s, j * P:(j + 1) * P],
                                dn_lo[:, s, j * P:(j + 1) * P], m_hi, m_lo, first and j % 2 == 0, last)
                    if last and j % 2 and j < KC - 1:
                        ins.then_inc(bank_done, 1)
                ins.then_inc(dn_done, 1)

            def norm(ph):
                for j in range(KC):
                    pe.wait_ge(sq_done, ph * KC + j + 1)
                    ins = nc.tensor.matmul(stat[:, 0:T], mean_w[:, :], sq[:, j, :], start=j == 0, stop=j == KC - 1)
                ins.then_inc(mean_done, 1)

            def ada_reduce(n):
                pe.wait_ge(ada_step, 8 * n + 8)
                if not isinstance(n, int) or n >= 1:
                    pe.wait_ge(ada_fin, n)
                for c in range(AC):
                    ins = nc.tensor.matmul(aux[:, c:c + 1], ada_sum[:, c * P:(c + 1) * P], ones_c[:, :],
                                           start=True, stop=True)
                ins.then_inc(ada_red, 1)

            def ada_start(n):
                last = n == N_ADA_START - 1
                if last:
                    slot, landed = start_slots[(2 * n + 1) % 4]
                    pe.wait_ge(landed, 16 * (n // 2 + 1))
                    for k in range(KH):
                        for c in range(AC):
                            nc.tensor.matmul(acc[n][:, c:c + 1], slot[:, k * AW + c * P:k * AW + (c + 1) * P],
                                             c_act[:, KH + k:KH + k + 1], start=k == 0 and c == 0, stop=False,
                                             skip_group_check=True)
                pe.wait_ge(ada_step, 8 * n + 8)
                for c in range(AC):
                    ins = nc.tensor.matmul(acc[n][:, c:c + 1], ada_total(n)[:, c * P:(c + 1) * P], ones_c[:, :],
                                           start=not last and c == 0, stop=True, skip_group_check=True)
                ins.then_inc(ada_red, 1)

            def ffn(ph, reduce_first):
                first, count = ADA_OF[ph]

                def up_f(f, s):
                    if not isinstance(f, int) or f >= 2:
                        pe.wait_ge(prod_done, FFN_NUMBER[ph] * NF + f - 1)
                    up(ph, f, s, isinstance(f, int) and f == 0)

                def down_f(f, s, **kw):
                    pe.wait_ge(al_done, AH0[ph] + f + 1)
                    down(D0[ph] + f, s, a_hi[:, s, :], a_lo[:, s, :], **kw)

                if ph != FFN0:
                    norm(ph)
                up_f(0, 0)
                if reduce_first:
                    ada_reduce(first - 1)
                up_f(1, 1)
                down_f(0, 0, first=True)
                last = NF // 2 - 1

                def body(i, reduce):
                    up_f(2 * i, 0)
                    if reduce:
                        ada_reduce(first + i - 1)
                    down_f(2 * i - 1, 1)
                    up_f(2 * i + 1, 1)
                    down_f(2 * i, 0)
                stop = min(last, count) if count else last
                with pe.Fori(1, stop) as i:
                    body(i, count > 0)
                for i in range(stop, last):
                    body(i, i == count)
                up_f(NF - 2, 0)
                if count > last:
                    ada_reduce(first + last - 1)
                down_f(NF - 3, 1)
                up_f(NF - 1, 1)
                down_f(NF - 2, 0)
                down_f(NF - 1, 1, last=True)

            pe.wait_ge(cv_pad, 1)
            pe.wait_ge(c_done, 1)
            for n in range(N_ADA_START):
                ada_start(n)
                if n == 1:
                    pe.wait_ge(mean_w_in, 16)
                    norm(FFN0)
            ffn(FFN0, False)
            pe.wait_ge(consts_in, 16 * N_CONST_DMAS)

            def head_norm(n):
                pe.wait_ge(squared, n + 1)
                if n:
                    pe.wait_ge(head_rstd, 2 * n - 1)
                for t in range(2):
                    ins = nc.tensor.matmul(stat[:, 0:T], head_w[:, :], qk_sq[:, t * T:(t + 1) * T],
                                           start=t == 0, stop=t == 1)
                ins.then_inc(head_mean, 1)

            def scores(r):
                pe.wait_ge(rot_done, r + 2)
                q = q_rot[:, r % 2, :]
                for g in range(KV):
                    if KV * r + g >= 2:
                        pe.wait_ge(masked, KV * r + g - 1)
                    rows = slice(g * HALF, (g + 1) * HALF)
                    for b in range(2):
                        out = acc[g % 2][:, b * P:S_COLS if b else P]
                        for t in range(2):
                            ins = nc.tensor.matmul(out, q[rows, t * T + b * P:t * T + (b + 1) * P],
                                                   k_rot[rows, t * T:t * T + (b + 1) * P],
                                                   start=t == 0, stop=t == 1)
                    ins.then_inc(scored, 1)

            def turn(r, g):
                n = KV * r + g
                pe.wait_ge(norm_done, 2 * n + 2)
                if n >= 2:
                    pe.wait_ge(pt_done, n - 1)
                for c in range(3):
                    ins = nc.tensor.transpose(acc[2 + g % 2][:, c * P:(c + 1) * P],
                                              probs[:, r % 2, g, c * P:(c + 1) * P], ident[:, :])
                ins.then_inc(pt_ready, 1)

            def weigh(r, g):
                n = KV * r + g
                pe.wait_ge(pt_done, n + 1)
                if n == 0:
                    pe.wait_ge(v_done, 2)
                    pe.wait_ge(ada_fin, ADA_ATTN + 1)
                if g % 2 == 0 and n:
                    pe.wait_ge(of_done, n // 2)
                rows = slice((g % 2) * HD, (g % 2 + 1) * HD)
                for b, c, start, stop in ((0, 0, True, True), (0, 1, True, False), (1, 2, False, True)):
                    q = 0 if c == 0 else P
                    ins = nc.tensor.matmul(aux[rows, q:q + P], v_sb[:, b, g * HD:(g + 1) * HD],
                                           p_t[:, g % 2, c * P:(c + 1) * P], start=start, stop=stop)
                ins.then_inc(pv_done, 1)

            def heads(r):
                turn(r, 0)
                for g in range(KV):
                    if g + 1 < KV:
                        turn(r, g + 1)
                    weigh(r, g)

            norm(ATTN)
            up(ATTN, 0, 0, True)
            pe.wait_ge(up_lo_done, U0[ATTN] + 2)
            for b in range(2):
                for k in range(KC):
                    at = 2 * k * P
                    blk = slice(b * P, (b + 1) * P)
                    out = pair[1][:, b * T:(b + 1) * T]
                    nc.tensor.matmul(out, h_hi[:, k, blk], up_hi[:, 1, at:at + T], start=k == 0, stop=False,
                                     skip_group_check=True)
                    nc.tensor.matmul(out, h_lo[:, k, blk], up_hi[:, 1, at:at + T], start=False, stop=False,
                                     skip_group_check=True)
                    ins = nc.tensor.matmul(out, h_hi[:, k, blk], up_lo[:, 1, at:at + T], start=False, stop=k == KC - 1,
                                           skip_group_check=True)
            ins.then_inc(up_done, 1)
            ada_reduce(ADA_ATTN - 1)
            head_norm(0)
            pe.wait_ge(biased, 2)
            up(ATTN, 2, 0)
            head_norm(1)
            for r in range(GROUP):
                if r < GROUP - 1:
                    if r == 0:
                        pe.wait_ge(v_done, 2)
                    else:
                        pe.wait_ge(biased, 2 * r + 2)
                    up(ATTN, r + 3, (r + 3) % 2)
                scores(r)
                if r < GROUP - 1:
                    head_norm(r + 2)
                if r == 0:
                    ada_reduce(ADA_ATTN)
                if r:
                    heads(r - 1)
            heads(GROUP - 1)
            pe.wait_ge(masked, KV * GROUP)
            pe.wait_ge(pt_done, KV * GROUP)
            for t in range(KC):
                pe.wait_ge(ol_done, t + 1)
                down(D0[ATTN] + t, t % 2, o_hi[:, t, :], o_lo[:, t, :], first=t == 0, last=t == KC - 1)

            ffn(FFN1, False)
            ffn(FFN2, True)

            norm(CONV)

            def down_pair(i):
                for s in range(2):
                    t = 2 * i + s
                    pe.wait_ge(al_done, AH0[CONV] + t + 1)
                    down(D0[CONV] + t, s, a_hi[:, s, :], a_lo[:, s, :], first=t == 0, last=t == KC - 1)
            for i in range(KC // 2):
                for s in range(3):
                    u = 3 * i + s
                    if u >= 2:
                        v = u - 2
                        if v % 3 == 2:
                            pe.wait_ge(cv_step, 10 * (v // 3) + 10)
                        else:
                            pe.wait_ge(cv_in, 2 * (v // 3) + v % 3 + 1)
                    up(CONV, u, u % 2, u == 0)
                if i:
                    down_pair(i - 1)
            down_pair(KC // 2 - 1)
            ffn(FFN3, False)


AH0 = {FFN0: 0, FFN1: NF, FFN2: 2 * NF, CONV: 3 * NF, FFN3: 3 * NF + KC}


def kernel(x, c, positions, norm_gain, w_ada, b_ada, w_ffn_up, w_ffn_down, attn_w_qkv, attn_b_qkv,
           attn_q_gain, attn_k_gain, attn_sinks, attn_w_o, attn_b_o, conv_w_in, conv_w, conv_w_out):
    import concourse.bacc as bacc
    from concourse.bass_utils import run_bass_kernel_spmd as run

    f32 = np.float32

    def chunks(v):
        return np.asarray(v).reshape(-1, KC, P).transpose(2, 0, 1).reshape(P, -1)

    bq = np.asarray(attn_b_qkv)[0, :HEADS * HD].reshape(KV, GROUP, 2, HALF)
    bk = np.asarray(attn_b_qkv)[0, HEADS * HD:(HEADS + KV) * HD].reshape(KV, 2, HALF)
    v_at = (HEADS + KV) * HD

    def per_half(g):
        return np.broadcast_to(np.asarray(g)[0].reshape(1, 2, HALF).transpose(0, 2, 1), (KV, HALF, 2)).reshape(P, 2)

    sinks = np.asarray(attn_sinks)[0].reshape(KV, GROUP).transpose(1, 0)
    sinks = np.broadcast_to(sinks[None, :, None, :], (P, GROUP, 2, KV)).reshape(P, -1)
    inv = (f32(10000.0) ** (-np.arange(0, HD, 2, dtype=f32) / f32(HD))).astype(f32)
    parts = {
        "c": chunks(c), "gain": chunks(norm_gain), "b_ada": chunks(b_ada), "conv_w": chunks(conv_w), "b_o": chunks(attn_b_o),
        "b_q": bq.transpose(0, 3, 1, 2).reshape(P, -1), "b_k": bk.transpose(0, 2, 1).reshape(P, -1),
        "q_gain": per_half(attn_q_gain), "k_gain": per_half(attn_k_gain), "sinks": sinks,
        "inv_freq": np.tile(inv, KV)[:, None], "half_pi": np.full((P, 1), math.pi / 2, f32),
        "eps": np.full((P, 1), EPS, f32),
    }
    cols = np.concatenate([parts[n] for n in COLS], axis=1)
    q = np.arange(P)[:, None]
    mask = np.zeros((P, S_COLS), f32)
    mask[:, :P][q < np.arange(P)[None]] = MASKED
    rel = P + q - np.arange(2 * P)[None]
    mask[:, P:][(rel < 0) | (rel >= P)] = MASKED
    w_qkv = np.asarray(attn_w_qkv)[0].reshape(KC, P, -1)
    wq = w_qkv[:, :, :HEADS * HD].reshape(KC, P, KV, GROUP, 2, HALF).transpose(3, 1, 0, 4, 2, 5).reshape(GROUP, P, UP)
    wk = w_qkv[:, :, HEADS * HD:v_at].reshape(KC, P, KV, 2, HALF).transpose(1, 0, 3, 2, 4).reshape(1, P, UP)
    wv = w_qkv[:, :, v_at:].transpose(1, 0, 2).reshape(1, P, UP)
    w_in = np.asarray(conv_w_in)[0].reshape(KC, P, 3, KC // 2, 2, P)
    cv = w_in[:, :, 1:].transpose(3, 4, 1, 0, 2, 5).reshape(KC // 2, 2, P, UP)
    gb = w_in[:, :, 0].transpose(2, 1, 0, 3, 4).reshape(KC // 2, 1, P, UP)
    arrays = {
        "x_t": np.asarray(x)[0].T,
        "cols_d": cols,
        "pos_d": np.asarray(positions)[0],
        "bv_d": np.asarray(attn_b_qkv)[0, v_at:],
        "ident_d": np.eye(P, dtype=f32),
        "ones_d": np.full((P, P), 1 / D, f32),
        "heads_d": np.kron(np.eye(KV, dtype=f32), np.full((HALF, HALF), 1 / HD, f32)),
        "mask_d": mask,
        "w_ada_d": np.asarray(w_ada).reshape(2, 2, KH, P, -1, AW).transpose(0, 4, 1, 3, 2, 5).reshape(-1, P, KH * AW),
        "w_up_d": np.asarray(w_ffn_up).reshape(4, KC, P, 2, NF, P).transpose(0, 4, 2, 1, 3, 5).reshape(-1, P, UP),
        "w_down_d": np.asarray(w_ffn_down).reshape(-1, P, DN),
        "w_qkv_d": np.concatenate([wk, wv, wq]),
        "w_o_d": np.asarray(attn_w_o)[0].reshape(2, 2, GROUP, HD, D).transpose(2, 0, 1, 3, 4).reshape(KC, P, D),
        "w_cin_d": np.concatenate([cv, gb], axis=1).reshape(-1, P, UP),
        "w_cout_d": np.asarray(conv_w_out)[0].reshape(KC, P, D),
    }
    arrays = {n: np.ascontiguousarray(a) for n, a in arrays.items()}
    nc = bacc.Bacc("TRN2", target_bir_lowering=False, num_devices=1)
    aps = [nc.dram_tensor(n, a.shape, mybir.dt.from_np(a.dtype), kind="ExternalInput").ap() for n, a in arrays.items()]
    aps.append(nc.dram_tensor("out_t", (D, T), F32, kind="ExternalOutput").ap())
    build(nc, *aps)
    r = run(nc, [arrays], core_ids=[0])
    return r.results[0]["out_t"].T.reshape(1, T, D)
```

```python
from contextlib import ExitStack
import math

import numpy as np

import concourse.bass as bass
from concourse import mybir
from concourse.alu_op_type import AluOpType as ALU

F32 = mybir.dt.float32
F32R = mybir.dt.float32r
I32 = mybir.dt.int32
ACT = mybir.ActivationFunctionType
AX = mybir.AxisListType

P = 128
D = 1024
T = 256
KC = D // P
FF = 2816
NF = FF // P
HEADS, KV, HD = 16, 4, 64
GROUP = HEADS // KV
HALF = HD // 2
EPS = 1e-6
N_ADA = 9
UP = 2 * KC * P
DN = D
AC = 4
AH = AC // 2
ADA_UNITS = 2 * N_ADA * KC // AC
N_ADA_START = 2 * KC // AC
MASKED = -3.0e38

FFN0, ATTN, FFN1, FFN2, CONV, FFN3 = range(6)
UPS = [NF, 6, NF, NF, 12, NF]
DOWNS = [NF, KC, NF, NF, KC, NF]
U0 = [sum(UPS[:n]) for n in range(6)]
D0 = [sum(DOWNS[:n]) for n in range(6)]
N_UP, N_DOWN = sum(UPS), sum(DOWNS)
FFN_NUMBER = {FFN0: 0, FFN1: 1, FFN2: 2, FFN3: 3}
ADA_OF = {FFN0: (N_ADA_START, NF // 2)}
ADA_ATTN = N_ADA_START + NF // 2
ADA_OF[FFN1] = (ADA_ATTN + 1, NF // 2)
ADA_OF[FFN2] = (ADA_ATTN + 1 + NF // 2, ADA_UNITS - (ADA_ATTN + 1 + NF // 2))
ADA_OF[FFN3] = (ADA_UNITS, 0)

COLS = {}
_at = 0
for _name, _n in (("gain", 6 * KC), ("b_ada", 2 * N_ADA * KC), ("conv_w", 3 * KC), ("b_o", KC),
                  ("b_q", 2 * GROUP), ("b_k", 2), ("q_gain", 2), ("k_gain", 2), ("sinks", GROUP * 2 * KV),
                  ("inv_freq", 1), ("half_pi", 1), ("eps", 1)):
    COLS[_name] = (_at, _at + _n)
    _at += _n
N_COLS = _at
S_COLS = 3 * P


def build(nc, x_t, c_d, cols_d, pos_d, bv_d, ident_d, ones_d, heads_d, mask_d, w_ada, w_up, w_down, w_qkv, w_o,
          w_cin, w_cout, out_t):
    up_of = [w_up, w_qkv, w_up, w_up, w_cin, w_up]
    down_of = [w_down, w_o, w_down, w_down, w_cout, w_down]

    def first_row(ph):
        return FFN_NUMBER[ph] * NF if ph in FFN_NUMBER else 0

    with ExitStack() as ctx:
        def sb(name, shape, dt=F32):
            return ctx.enter_context(nc.sbuf_tensor(name, shape, dt))

        def sem(name):
            return ctx.enter_context(nc.semaphore(name))

        up_raw = sb("up_raw", [P, 2, UP])
        up_hi = sb("up_hi", [P, 2, UP], F32R)
        up_lo = sb("up_lo", [P, 2, UP], F32R)
        dn_raw = sb("dn_raw", [P, 2, DN])
        dn_hi = sb("dn_hi", [P, 2, DN], F32R)
        dn_lo = sb("dn_lo", [P, 2, DN], F32R)
        ada_raw = sb("ada_raw", [P, 2, AH * D])
        ada_out = sb("ada_out", [P, 4 * AH])
        mod = sb("mod", [P, 2 * N_ADA * KC])
        cols = sb("cols", [P, N_COLS])
        c_row = sb("c_row", [P, D])
        ident = sb("ident", [P, P])
        mean_w = sb("mean_w", [P, P])
        head_w = sb("head_w", [P, P])
        mask = sb("mask", [P, S_COLS])
        pos = sb("pos", [P, T], I32)
        bv = sb("bv", [P, KV * HD])
        cos2 = sb("cos2", [P, 2 * T])
        sin2 = sb("sin2", [P, 2 * T])
        x = sb("x", [P, KC, T])
        sq = sb("sq", [P, KC, T])
        xs = sb("xs", [P, KC, T])
        h_hi = sb("h_hi", [P, KC, T], F32R)
        h_lo = sb("h_lo", [P, KC, T], F32R)
        ln_ms = sb("ln_ms", [P, T])
        rstd = sb("rstd", [P, T])
        a_col = sb("a_col", [P, KC])
        g_col = sb("g_col", [P, KC])
        gb_col = sb("gb_col", [P, KC])
        gate_s = sb("gate_s", [P, 2, T])
        prod = sb("prod", [P, 2, T])
        a_hi = sb("a_hi", [P, 2, T], F32R)
        a_lo = sb("a_lo", [P, 2, T], F32R)
        qk_t = sb("qk_t", [P, 2 * T])
        qk_sq = sb("qk_sq", [P, 2 * T])
        qk_n = sb("qk_n", [P, 2 * T])
        qk_c = sb("qk_c", [P, 2 * T])
        qk_s = sb("qk_s", [P, 2 * T])
        ang = qk_c[:, :].rearrange("p (a t) -> p a t", a=2)
        qk_r = sb("qk_r", [P, T])
        k_rot = xs
        q_rot = sb("q_rot", [P, 2, 2 * T])
        v_sb = sb("v_sb", [P, 2, KV * HD])
        probs = sb("probs", [P, 2, KV, S_COLS])
        m_col = sb("m_col", [P, 2, 2 * KV])
        nm_col = sb("nm_col", [P, 2, 2 * KV])
        sd_col = sb("sd_col", [P, 2, 2 * KV])
        es_col = sb("es_col", [P, 2, 2 * KV])
        su_col = sb("su_col", [P, 2, 2 * KV])
        de_col = sb("de_col", [P, 2, 2 * KV])
        ri_col = sb("ri_col", [P, 2, 2 * KV])
        p_t = sb("p_t", [P, 2, S_COLS])
        o_hi = sb("o_hi", [P, KC, T], F32R)
        o_lo = sb("o_lo", [P, KC, T], F32R)
        cv_u = sb("cv_u", [P, 2, 2 + T])
        cv_y = sb("cv_y", [P, 2, T])

        acc = [ctx.enter_context(nc.psum_tensor(f"acc{n}", [P, 2 * T], F32)) for n in range(4)]
        pair = [ctx.enter_context(nc.psum_tensor(f"pair{n}", [P, 2 * T], F32)) for n in range(2)]
        stat = ctx.enter_context(nc.psum_tensor("stat", [P, 2 * T], F32))
        aux = ctx.enter_context(nc.psum_tensor("aux", [P, 2 * T], F32))

        o_bank = (aux, pair[0])

        consts_in = sem("consts_in")
        x_in = sem("x_in")
        up_in = [sem(f"up_in{n}") for n in range(2)]
        dn_in = [sem(f"dn_in{n}") for n in range(2)]
        ada_in = [sem(f"ada_in{n}") for n in range(2)]
        c_in, cols_in, pos_in, mean_w_in = sem("c_in"), sem("cols_in"), sem("pos_in"), sem("mean_w_in")
        start_in = [sem(f"start_in{n}") for n in range(2)]
        stored = sem("stored")
        up_hi_done, up_lo_done = sem("up_hi_done"), sem("up_lo_done")
        dn_hi_done, dn_lo_done = sem("dn_hi_done"), sem("dn_lo_done")
        up_done, dn_done = sem("up_done"), sem("dn_done")
        bank_done = sem("bank_done")
        c_done = sem("c_done")
        ada_step = sem("ada_step")
        mod_done = sem("mod_done")
        x_done, sq_done, mean_done, rstd_done = sem("x_done"), sem("sq_done"), sem("mean_done"), sem("rstd_done")
        ln_done, xs_done, hh_done, h_done = sem("ln_done"), sem("xs_done"), sem("hh_done"), sem("h_done")
        col_step = sem("col_step")
        gate_done, prod_done, ah_done, al_done = sem("gate_done"), sem("prod_done"), sem("ah_done"), sem("al_done")
        tab_step, tab_done = sem("tab_step"), sem("tab_done")
        biased, squared, head_mean, head_rstd, rope_step, rot_done = (sem(n) for n in (
            "biased", "squared", "head_mean", "head_rstd", "rope_step", "rot_done"))
        v_done, scored, masked, soft_step, exp_done, norm_done = (sem(n) for n in (
            "v_done", "scored", "masked", "soft_step", "exp_done", "norm_done"))
        pt_ready, pt_done, pv_done, oh_done, ol_done = (sem(n) for n in (
            "pt_ready", "pt_done", "pv_done", "oh_done", "ol_done"))
        k_zero = sem("k_zero")
        cv_c, cv_in, cv_step, cv_pad = sem("cv_c"), sem("cv_in"), sem("cv_step"), sem("cv_pad")

        def col(name, a=0, n=None):
            lo, hi = COLS[name]
            return cols[:, lo + a:hi if n is None else lo + a + n]

        def mod_cols(layer, v):
            at = (layer * N_ADA + v) * KC
            return mod[:, at:at + KC]

        N_CONST_DMAS = 4
        SOFT = 2 * KV + 3
        start_slots = [(ada_raw[:, 0, :], ada_in[0]), (ada_raw[:, 1, :], ada_in[1]),
                       (dn_raw[:, :, :].rearrange("p k t -> p (k t)"), start_in[0]),
                       (probs[:, :, :, :].rearrange("p a g n -> p (a g n)")[:, 0:AH * D], start_in[1])]
        start_halves = list(range(N_ADA_START, 2 * N_ADA_START)) + list(range(N_ADA_START))
        norm_of = {FFN0: (0, 0), ATTN: (0, 1), FFN1: (0, 2), FFN2: (1, 0), CONV: (1, 1), FFN3: (1, 2)}

        block = ctx.enter_context(nc.Block())

        @block.sync
        def _(sp):
            def load_up(ph, f, s):
                n = U0[ph] + f
                if not isinstance(n, int) or n >= 2:
                    sp.wait_ge(up_lo_done, n - 1)
                sp.dma_start(up_raw[:, s, :],
                             up_of[ph][bass.ds(first_row(ph) + f, 1), :, :].rearrange("a p n -> p (a n)")
                             ).then_inc(up_in[s], 16)

            def load_down(ph, f, s):
                n = D0[ph] + f
                if not isinstance(n, int) or n >= 2:
                    sp.wait_ge(dn_lo_done, n - 1)
                sp.dma_start(dn_raw[:, s, :],
                             down_of[ph][bass.ds(first_row(ph) + f, 1), :, :].rearrange("a p n -> p (a n)")
                             ).then_inc(dn_in[s], 16)

            def load_start(i):
                slot, landed = start_slots[i % 4]
                if i >= 4:
                    sp.wait_ge(ada_step, AH * (i - 3))
                sp.dma_start(slot, w_ada[start_halves[i], :, :]).then_inc(landed, 16)

            sp.dma_start(cols[:, :], cols_d).then_inc(cols_in, 16)
            sp.dma_start(pos[:, :], pos_d.partition_broadcast(P)).then_inc(pos_in, 16)
            sp.dma_start(c_row[:, :], c_d.partition_broadcast(P)).then_inc(c_in, 16)
            for i in range(4):
                load_start(i)
            sp.dma_start(x[:, :, :], x_t.rearrange("(k p) t -> p k t", p=P)).then_inc(x_in, 16)
            sp.dma_start(mean_w[:, :], ones_d).then_inc(mean_w_in, 16)
            for i in (4, 5):
                load_start(i)
            load_up(FFN0, 0, 0)
            for i in (6, 7):
                load_start(i)
            load_up(FFN0, 1, 1)
            sp.wait_ge(ada_step, AH * 7)
            load_down(FFN0, 0, 0)
            sp.dma_start(bv[:, :], bv_d.partition_broadcast(P)).then_inc(consts_in, 16)
            sp.dma_start(ident[:, :], ident_d).then_inc(consts_in, 16)
            sp.dma_start(head_w[:, :], heads_d).then_inc(consts_in, 16)
            sp.dma_start(mask[:, :], mask_d).then_inc(consts_in, 16)

            def ffn_loads(ph, ups_there=False):
                if not ups_there:
                    load_up(ph, 0, 0)
                    load_up(ph, 1, 1)
                if ph != FFN0:
                    load_down(ph, 0, 0)
                with sp.Fori(1, NF // 2) as i:
                    load_up(ph, 2 * i, 0)
                    load_down(ph, 2 * i - 1, 1)
                    load_up(ph, 2 * i + 1, 1)
                    load_down(ph, 2 * i, 0)
                load_down(ph, NF - 1, 1)

            ffn_loads(FFN0, ups_there=True)
            for kind, n in (("u", 0), ("d", 0), ("u", 1), ("u", 2), ("u", 3), ("d", 1), ("u", 4), ("u", 5), ("d", 2),
                            ("d", 3), ("next", 0), ("next", 1), ("d", 4), ("d", 5), ("d", 6), ("d", 7)):
                if kind == "next":
                    load_up(FFN1, n, n)
                else:
                    (load_up if kind == "u" else load_down)(ATTN, n, n % 2)
            ffn_loads(FFN1, ups_there=True)
            ffn_loads(FFN2)
            for i in range(4):
                load_up(CONV, 3 * i, (3 * i) % 2)
                if i:
                    load_down(CONV, 2 * i - 1, 1)
                load_up(CONV, 3 * i + 1, (3 * i + 1) % 2)
                load_up(CONV, 3 * i + 2, (3 * i + 2) % 2)
                load_down(CONV, 2 * i, 0)
            load_down(CONV, KC - 1, 1)
            ffn_loads(FFN3)
            for j in range(KC):
                sp.wait_ge(x_done, 6 * KC + j + 1 - KC)
                sp.dma_start(out_t[j * P:(j + 1) * P, :], x[:, j, :]).then_inc(stored, 16)
            sp.wait_ge(stored, 16 * KC)

        @block.scalar
        def _(act):
            def round_up(n, s):
                if isinstance(n, int) and n >= N_UP:
                    return
                act.wait_ge(up_in[s], 8 * (n - s) + 16)
                if not isinstance(n, int) or n >= 2:
                    act.wait_ge(up_done, n - 1)
                nc.scalar.activation(up_hi[:, s, :], up_raw[:, s, :], ACT.Copy).then_inc(up_hi_done, 1)

            def round_down(n, s):
                if isinstance(n, int) and n >= N_DOWN:
                    return
                act.wait_ge(dn_in[s], 8 * (n - s) + 16)
                if not isinstance(n, int) or n >= 2:
                    act.wait_ge(dn_done, n - 1)
                nc.scalar.activation(dn_hi[:, s, :], dn_raw[:, s, :], ACT.Copy).then_inc(dn_hi_done, 1)

            def load_half(n, s):
                if isinstance(n, int) and n >= ADA_UNITS:
                    return
                if isinstance(n, int) and n == N_ADA_START:
                    act.wait_ge(ada_step, AH * (5 + s))
                else:
                    act.wait_ge(ada_step, AC * (n - 1) + AH * (s + 1))
                act.dma_start(ada_raw[:, s, :],
                              w_ada[bass.ds(2 * n + s, 1), :, :].rearrange("a p n -> p (a n)")
                              ).then_inc(ada_in[s], 16)

            def norm_table():
                nc.scalar.preload_act_table_set("natural_log_exp_and_others")

            def squares(ph):
                if ph in (FFN0, FFN3):
                    norm_table()
                for j in range(KC):
                    if ph == FFN0:
                        if j == 0:
                            act.wait_ge(x_in, 16)
                    else:
                        act.wait_ge(x_done, (ph - 1) * KC + j + 1)
                    nc.scalar.activation(sq[:, j, :], x[:, j, :], ACT.Square).then_inc(sq_done, 1)

            def scale(ph):
                act.wait_ge(mean_done, ph + 1)
                nc.scalar.activation(ln_ms[:, :], stat[:, 0:T], ACT.Ln, bias=col("eps")).then_inc(ln_done, 1)
                act.wait_ge(ln_done, ph + 1)
                nc.scalar.activation(rstd[:, :], ln_ms[:, :], ACT.Exp, scale=-0.5).then_inc(rstd_done, 1)

            def shifted(ph):
                layer, sub = norm_of[ph]
                shift = mod_cols(layer, 3 * sub)
                for j in range(KC):
                    act.wait_ge(xs_done, ph * KC + j + 1)
                    if ph == FFN0:
                        act.wait_ge(mod_done, KC + j + 1)
                    nc.scalar.activation(h_hi[:, j, :], xs[:, j, :], ACT.Identity,
                                         bias=shift[:, j:j + 1]).then_inc(hh_done, 1)
                if ph in FFN_NUMBER:
                    nc.scalar.preload_act_table(ACT.Silu)

            def norm(ph):
                squares(ph)
                scale(ph)
                shifted(ph)

            def hidden(ph, f, s, last=False):
                g = FFN_NUMBER[ph] * NF + f
                act.wait_ge(up_done, U0[ph] + f + 1)
                nc.scalar.activation(gate_s[:, s, :], pair[s][:, 0:T], ACT.Silu).then_inc(gate_done, 1)
                if last and ph != FFN3:
                    norm_table()
                if not isinstance(f, int) or f >= 2:
                    act.wait_ge(dn_done, D0[ph] + f - 1)
                act.wait_ge(prod_done, g + 1)
                nc.scalar.activation(a_hi[:, s, :], prod[:, s, :], ACT.Copy).then_inc(ah_done, 1)

            def ffn(ph):
                first, count = ADA_OF[ph]

                def period(f, s, n):
                    hidden(ph, f, s)
                    round_up(U0[ph] + f + 2, s)
                    round_down(D0[ph] + f + 1, 1 - s)
                    if n is not None:
                        load_half(n + 1, s)
                last = NF // 2 - 1
                if ph != FFN0:
                    norm(ph)
                if ph in (FFN2, FFN3):
                    round_down(D0[ph], 0)
                stop = min(last, count - 1) if count else last
                period(0, 0, first if count else None)
                if ph == FFN2:
                    load_half(first, 1)
                period(1, 1, first if count else None)
                with act.Fori(1, stop) as i:
                    period(2 * i, 0, first + i if count else None)
                    period(2 * i + 1, 1, first + i if count else None)
                for i in range(stop, last):
                    period(2 * i, 0, first + i if i < count else None)
                    period(2 * i + 1, 1, first + i if i < count else None)
                period(NF - 2, 0, first + last if count > last else None)
                hidden(ph, NF - 1, 1, last=True)
                round_up(U0[ph] + NF + 1, 1)

            act.wait_ge(c_in, 16)
            nc.scalar.activation(c_row[:, :], c_row[:, :], ACT.Silu).then_inc(c_done, 1)
            act.wait_ge(cols_in, 16)
            act.wait_ge(tab_step, 8)
            for t in range(2):
                nc.scalar.activation(sin2[:, t * T:(t + 1) * T], ang[:, 0, :], ACT.Sin).then_inc(tab_done, 1)
                nc.scalar.activation(cos2[:, t * T:(t + 1) * T], ang[:, 1, :], ACT.Sin, scale=-1.0,
                                     bias=col("half_pi")).then_inc(tab_done, 1)
            squares(FFN0)
            scale(FFN0)
            load_half(N_ADA_START, 0)
            load_half(N_ADA_START, 1)
            round_up(0, 0)
            shifted(FFN0)
            round_up(1, 1)
            round_down(0, 0)
            ffn(FFN0)

            def bias_square(n, b):
                act.wait_ge(up_done, U0[ATTN] + (1 if n == 0 else n + 2))
                if n >= 1:
                    act.wait_ge(rope_step, 5 * n)
                for t in range(2):
                    ins = nc.scalar.activation(qk_t[:, t * T:(t + 1) * T], pair[(0 if n == 0 else n + 1) % 2][:, t * T:(t + 1) * T],
                                               ACT.Identity, bias=b[:, t:t + 1]).then_inc(biased, 1)
                act.wait_ge(biased, 2 * n + 2)
                nc.scalar.activation(qk_sq[:, :], qk_t[:, :], ACT.Square).then_inc(squared, 1)

            def head_scale(n):
                act.wait_ge(head_mean, n + 1)
                nc.scalar.activation(qk_r[:, :], stat[:, 0:T], ACT.Ln, bias=col("eps")).then_inc(head_rstd, 1)
                act.wait_ge(head_rstd, 2 * n + 1)
                nc.scalar.activation(qk_r[:, :], qk_r[:, :], ACT.Exp, scale=-0.5).then_inc(head_rstd, 1)

            def exps(r, g):
                s = r % 2
                if g == 0:
                    act.wait_ge(soft_step, SOFT * (r + 1))
                for b in range(2):
                    e = probs[:, s, g, 0:P] if b == 0 else probs[:, s, g, P:S_COLS]
                    nc.scalar.activation(e, e, ACT.Exp, bias=nm_col[:, s, b * KV + g:b * KV + g + 1],
                                         accum_out=su_col[:, s, b * KV + g:b * KV + g + 1]).then_inc(exp_done, 1)
                if g == KV - 1:
                    nc.scalar.activation(es_col[:, s, :], sd_col[:, s, :], ACT.Exp).then_inc(exp_done, 1)

            def output(r, g):
                n = KV * r + g
                act.wait_ge(pt_ready, n + 1)
                if n >= 2:
                    act.wait_ge(pv_done, n - 1)
                nc.scalar.activation(p_t[:, g % 2, :], acc[2 + g % 2][:, 0:S_COLS], ACT.Copy).then_inc(pt_done, 1)
                if g % 2:
                    t = 2 * r + g // 2
                    act.wait_ge(pv_done, n + 1)
                    nc.scalar.activation(o_hi[:, t, :], o_bank[t % 2][:, 0:T], ACT.Copy).then_inc(oh_done, 1)

            norm(ATTN)
            round_down(D0[ATTN], 0)
            bias_square(0, col("b_k"))
            round_up(U0[ATTN] + 2, 0)
            head_scale(0)
            round_up(U0[ATTN] + 3, 1)
            round_down(D0[ATTN] + 1, 1)
            bias_square(1, col("b_q", 0, 2))
            round_up(U0[ATTN] + 4, 0)
            load_half(ADA_ATTN, 1)
            head_scale(1)
            round_up(U0[ATTN] + 5, 1)
            bias_square(2, col("b_q", 2, 2))
            for r in range(GROUP):
                if r < GROUP - 1:
                    head_scale(r + 2)
                if r:
                    output(r - 1, 0)
                    output(r - 1, 1)
                    exps(r, 0)
                    output(r - 1, 2)
                    exps(r, 1)
                    output(r - 1, 3)
                    exps(r, 2)
                    exps(r, 3)
                else:
                    for g in range(KV):
                        exps(r, g)
                if r < GROUP - 2:
                    bias_square(r + 3, col("b_q", 2 * r + 4, 2))
                    round_up(U0[ATTN] + r + 6, r)
                    load_half(ADA_ATTN + 1, r)
            for g in range(KV):
                output(GROUP - 1, g)
            for t in range(KC - 1):
                round_down(D0[ATTN] + t + 2, t % 2)

            ffn(FFN1)
            ffn(FFN2)

            norm(CONV)
            round_down(D0[CONV], 0)
            for i in range(KC // 2):
                for s in range(2):
                    u = 3 * i + s
                    act.wait_ge(up_done, U0[CONV] + u + 1)
                    nc.scalar.activation(gate_s[:, s, :], pair[u % 2][:, 0:T], ACT.Copy).then_inc(cv_c, 1)
                    if i < KC // 2 - 1 or s == 0:
                        round_up(U0[CONV] + u + 2, u % 2)
                    else:
                        round_down(D0[CONV] + 2 * i, 0)
                    if s == 0 and i:
                        round_down(D0[CONV] + 2 * i - 1, 1)
                for s in range(2):
                    act.wait_ge(cv_step, 10 * i + 2 * s + 8)
                    nc.scalar.activation(o_hi[:, 2 * i + s, :], cv_y[:, s, :], ACT.Copy).then_inc(ah_done, 1)
                if i < KC // 2 - 1:
                    round_up(U0[CONV] + 3 * i + 4, (3 * i + 4) % 2)
                    if i:
                        round_down(D0[CONV] + 2 * i, 0)
            round_down(D0[CONV] + KC - 1, 1)
            for n in range(2):
                round_up(U0[FFN3] + n, n)
            ffn(FFN3)

        @block.vector
        def _(dve):
            def rest_up(n, s):
                if isinstance(n, int) and n >= N_UP:
                    return
                dve.wait_ge(up_hi_done, n + 1)
                nc.vector.tensor_tensor(up_lo[:, s, :], up_raw[:, s, :], up_hi[:, s, :].bitcast(F32),
                                        ALU.subtract).then_inc(up_lo_done, 1)

            def rest_down(n, s):
                if isinstance(n, int) and n >= N_DOWN:
                    return
                dve.wait_ge(dn_hi_done, n + 1)
                nc.vector.tensor_tensor(dn_lo[:, s, :], dn_raw[:, s, :], dn_hi[:, s, :].bitcast(F32),
                                        ALU.subtract).then_inc(dn_lo_done, 1)

            def ada_sum(slot, at, k, before):
                if not isinstance(before, int) or before >= 4:
                    dve.wait_ge(mod_done, AH * (before - 3))
                w = slot[:, k * D:(k + 1) * D]
                nc.vector.tensor_tensor_reduce(out=w, in0=w, in1=c_row[:, :], scale=1.0, scalar=0.0,
                                               op0=ALU.mult, op1=ALU.add,
                                               accum_out=ada_out[:, AH * at + k:AH * at + k + 1]).then_inc(ada_step, 1)

            def keep(at, chunk, done):
                dve.wait_ge(ada_step, AH * done)
                nc.vector.tensor_tensor(mod[:, bass.ds(chunk, AH)], ada_out[:, AH * at:AH * (at + 1)],
                                        cols[:, bass.ds(COLS["b_ada"][0] + chunk, AH)], ALU.add
                                        ).then_inc(mod_done, AH)

            def ada_half(n, s):
                dve.wait_ge(ada_in[s], 16 * (n - 1))
                for k in range(AH):
                    ada_sum(ada_raw[:, s, :], s, k, 2 * n + s)
                keep(s, AC * n + AH * s, 2 * n + s + 1)

            small = [0]

            def column(ins):
                ins.then_inc(col_step, 1)
                small[0] += 1
                dve.wait_ge(col_step, small[0])

            def scale_column(ph):
                layer, sub = norm_of[ph]
                column(nc.vector.scalar_tensor_tensor(
                    out=a_col[:, :], in0=mod_cols(layer, 3 * sub + 1), scalar=1.0,
                    in1=col("gain", (3 * layer + sub) * KC, KC), op0=ALU.add, op1=ALU.mult))

            def prepare(ph, units):
                dve.wait_ge(mod_done, AC * units)
                scale_column(ph)

            def gate_column(ph):
                layer, sub = norm_of[ph]
                dve.wait_ge(mod_done, (layer * N_ADA + 3 * sub + 3) * KC)
                column(nc.vector.tensor_scalar(g_col[:, :], mod_cols(layer, 3 * sub + 2),
                                               0.5 if ph in FFN_NUMBER else 1.0, None, ALU.mult))

            def add_output(ph):
                for j in range(KC):
                    if j % 2 == 0 and j < KC - 2:
                        dve.wait_ge(bank_done, 3 * ph + j // 2 + 1)
                    elif j == KC - 2:
                        dve.wait_ge(dn_done, D0[ph] + DOWNS[ph])
                    nc.vector.scalar_tensor_tensor(out=x[:, j, :], in0=acc[j // 2][:, (j % 2) * T:(j % 2 + 1) * T],
                                                   scalar=g_col[:, j:j + 1], in1=x[:, j, :],
                                                   op0=ALU.mult, op1=ALU.add).then_inc(x_done, 1)

            def scale_chunk(ph, j):
                nc.vector.scalar_tensor_tensor(out=xs[:, j, :], in0=x[:, j, :], scalar=a_col[:, j:j + 1],
                                               in1=rstd[:, :], op0=ALU.mult, op1=ALU.mult).then_inc(xs_done, 1)

            def scaled(ph):
                dve.wait_ge(rstd_done, ph + 1)
                for j in range(KC):
                    scale_chunk(ph, j)

            def shifted_rest(ph, j):
                layer, sub = norm_of[ph]
                if ph == FFN0:
                    dve.wait_ge(mod_done, KC + j + 1)
                dve.wait_ge(hh_done, ph * KC + j + 1)
                nc.vector.scalar_tensor_tensor(out=h_lo[:, j, :], in0=xs[:, j, :],
                                               scalar=mod_cols(layer, 3 * sub)[:, j:j + 1],
                                               in1=h_hi[:, j, :].bitcast(F32), op0=ALU.add,
                                               op1=ALU.subtract).then_inc(h_done, 1)

            def norm(ph):
                dve.wait_ge(rstd_done, ph + 1)
                for j in range(KC):
                    scale_chunk(ph, j)
                    if j:
                        shifted_rest(ph, j - 1)
                shifted_rest(ph, KC - 1)

            def hidden(ph, f, s):
                g = FFN_NUMBER[ph] * NF + f
                dve.wait_ge(gate_done, g + 1)
                nc.vector.tensor_tensor(prod[:, s, :], gate_s[:, s, :], pair[s][:, T:2 * T], ALU.mult).then_inc(prod_done, 1)
                dve.wait_ge(ah_done, AH0[ph] + f + 1)
                nc.vector.tensor_tensor(a_lo[:, s, :], prod[:, s, :], a_hi[:, s, :].bitcast(F32),
                                        ALU.subtract).then_inc(al_done, 1)

            def ffn(ph, rest_first=False, then=None):
                first, count = ADA_OF[ph]
                if ph != FFN0:
                    norm(ph)
                if rest_first:
                    rest_down(D0[ph], 0)

                def period(f, s, n):
                    hidden(ph, f, s)
                    if isinstance(f, int) and f == 0 and PENDING_HALF[ph] is not None:
                        ada_half(PENDING_HALF[ph], 1)
                    if n is not None:
                        ada_half(n, s)
                    rest_up(U0[ph] + f + 2, s)
                    rest_down(D0[ph] + f + 1, 1 - s)

                last = NF // 2 - 1
                period(0, 0, first if count else None)
                period(1, 1, first if count else None)
                with dve.Fori(1, min(last, count) if count else last) as i:
                    period(2 * i, 0, first + i if count else None)
                    period(2 * i + 1, 1, first + i if count else None)
                for f in range(2 * min(last, count) if count else 2 * last, 2 * last):
                    period(f, f % 2, None)
                period(NF - 2, 0, first + last if count > last else None)
                gate_column(ph)
                if then:
                    prepare(*then)
                hidden(ph, NF - 1, 1)
                add_output(ph)
                rest_up(U0[ph] + NF + 1, 1)

            PENDING_HALF = {ph: None for ph in ADA_OF}
            PENDING_HALF[FFN2] = ADA_OF[FFN1][0] + NF // 2 - 1

            nc.vector.memset(cv_u[:, :, 0:2], 0.0).then_inc(cv_pad, 1)
            dve.wait_ge(cols_in, 16)
            dve.wait_ge(pos_in, 16)
            two_pi = 2 * math.pi
            part1 = 6.28125
            part2 = float(np.float32(round((two_pi - part1) * 2 ** 19) / 2 ** 19))
            part3 = float(np.float32(two_pi - part1 - part2))
            magic = 1.5 * 2 ** 23
            steps = [0]

            def angle(ins):
                ins.then_inc(tab_step, 1)
                steps[0] += 1
                dve.wait_ge(tab_step, steps[0])
            angle(nc.vector.tensor_scalar(ang[:, 0, :], pos[:, :], col("inv_freq"), None, ALU.mult))
            angle(nc.vector.tensor_scalar(ang[:, 1, :], ang[:, 0, :], 1 / two_pi, magic, ALU.mult, ALU.add))
            angle(nc.vector.tensor_scalar(ang[:, 1, :], ang[:, 1, :], magic, None, ALU.subtract))
            for part in (part1, part2, part3):
                angle(nc.vector.scalar_tensor_tensor(out=ang[:, 0, :], in0=ang[:, 1, :], scalar=-part, in1=ang[:, 0, :],
                                                     op0=ALU.mult, op1=ALU.add))
            pi = float(np.nextafter(np.float32(math.pi), np.float32(0)))
            angle(nc.vector.tensor_scalar(ang[:, 0, :], ang[:, 0, :], pi, -pi, ALU.min, ALU.max))
            angle(nc.vector.scalar_tensor_tensor(out=ang[:, 1, :], in0=ang[:, 0, :], scalar=-1.0, in1=ang[:, 0, :],
                                                 op0=ALU.mult, op1=ALU.max))

            dve.wait_ge(c_done, 1)

            def start_half(i):
                slot, landed = start_slots[i % 4]
                dve.wait_ge(landed, 16 * (i // 4 + 1))
                for k in range(AH):
                    ada_sum(slot, i % 4, k, i)
                keep(i % 4, AH * start_halves[i], i + 1)

            for i in range(4):
                start_half(i)
            dve.wait_ge(mod_done, KC)
            scale_column(FFN0)
            for i in (4, 5):
                start_half(i)
            scaled(FFN0)
            rest_up(0, 0)
            for i in (6, 7):
                start_half(i)
                for j in range(AH * (i - 6), AH * (i - 5)):
                    shifted_rest(FFN0, j)
            for j in range(2 * AH, KC):
                shifted_rest(FFN0, j)
            rest_up(1, 1)
            rest_down(0, 0)
            ffn(FFN0, then=(ATTN, N_ADA_START + 8))

            rope = [0]

            def rotate(n, gain, dst):
                def step(ins):
                    ins.then_inc(rope_step, 1)
                    rope[0] += 1
                dve.wait_ge(head_rstd, 2 * n + 2)
                for t in range(2):
                    step(nc.vector.scalar_tensor_tensor(out=qk_n[:, t * T:(t + 1) * T], in0=qk_t[:, t * T:(t + 1) * T],
                                                        scalar=gain[:, t:t + 1], in1=qk_r[:, :],
                                                        op0=ALU.mult, op1=ALU.mult))
                dve.wait_ge(rope_step, rope[0])
                step(nc.vector.tensor_tensor(qk_c[:, :], qk_n[:, :], cos2[:, :], ALU.mult))
                step(nc.vector.tensor_tensor(qk_s[:, :], qk_n[:, :], sin2[:, :], ALU.mult))
                dve.wait_ge(rope_step, rope[0])
                if dst is not k_rot:
                    step(nc.vector.tensor_tensor(dst[:, 0:T], qk_c[:, 0:T], qk_s[:, T:2 * T], ALU.subtract))
                    nc.vector.tensor_tensor(dst[:, T:2 * T], qk_c[:, T:2 * T], qk_s[:, 0:T], ALU.add).then_inc(rot_done, 1)
                    return
                dve.wait_ge(k_zero, 1)
                for g in range(KV):
                    rows = slice(g * HALF, (g + 1) * HALF)
                    first = nc.vector.tensor_tensor(k_rot[rows, g, :], qk_c[rows, 0:T], qk_s[rows, T:2 * T], ALU.subtract)
                    second = nc.vector.tensor_tensor(k_rot[rows, KV + g, :], qk_c[rows, T:2 * T], qk_s[rows, 0:T], ALU.add)
                step(first)
                second.then_inc(rot_done, 1)

            def softmax_columns(r):
                s = r % 2
                for g in range(KV):
                    dve.wait_ge(scored, KV * r + g + 1)
                    nc.vector.scalar_tensor_tensor(out=probs[:, s, g, :], in0=acc[g % 2][:, 0:S_COLS], scalar=HD ** -0.5,
                                                   in1=mask[:, :], op0=ALU.mult, op1=ALU.add).then_inc(masked, 1)
                    dve.wait_ge(masked, KV * r + g + 1)
                    nc.vector.tensor_reduce(m_col[:, s, g:g + 1], probs[:, s, g, 0:P], AX.X, ALU.max).then_inc(soft_step, 1)
                    nc.vector.tensor_reduce(m_col[:, s, KV + g:KV + g + 1], probs[:, s, g, P:S_COLS], AX.X,
                                            ALU.max).then_inc(soft_step, 1)
                dve.wait_ge(soft_step, SOFT * r + 2 * KV)
                sink = col("sinks", r * 2 * KV, 2 * KV)
                nc.vector.tensor_tensor(m_col[:, s, :], m_col[:, s, :], sink, ALU.max).then_inc(soft_step, 1)
                dve.wait_ge(soft_step, SOFT * r + 2 * KV + 1)
                nc.vector.tensor_scalar(nm_col[:, s, :], m_col[:, s, :], -1.0, None, ALU.mult).then_inc(soft_step, 1)
                nc.vector.tensor_tensor(sd_col[:, s, :], sink, m_col[:, s, :], ALU.subtract).then_inc(soft_step, 1)

            def normalise(r):
                s = r % 2
                dve.wait_ge(exp_done, 9 * r + 9)
                column(nc.vector.tensor_tensor(de_col[:, s, :], su_col[:, s, :], es_col[:, s, :], ALU.add))
                column(nc.vector.reciprocal(ri_col[:, s, :], de_col[:, s, :]))
                for g in range(KV):
                    for b in range(2):
                        e = probs[:, s, g, 0:P] if b == 0 else probs[:, s, g, P:S_COLS]
                        nc.vector.tensor_scalar(e, e, ri_col[:, s, b * KV + g:b * KV + g + 1], None,
                                                ALU.mult).then_inc(norm_done, 1)

            def rest_outputs(r):
                for t in (2 * r, 2 * r + 1):
                    dve.wait_ge(oh_done, t + 1)
                    nc.vector.tensor_tensor(o_lo[:, t, :], o_bank[t % 2][:, 0:T], o_hi[:, t, :].bitcast(F32),
                                            ALU.subtract).then_inc(ol_done, 1)

            norm(ATTN)
            dve.wait_ge(consts_in, 16 * N_CONST_DMAS)
            rest_down(D0[ATTN], 0)
            rest_up(U0[ATTN] + 2, 0)
            rotate(0, col("k_gain"), k_rot)
            rest_up(U0[ATTN] + 3, 1)
            dve.wait_ge(up_done, U0[ATTN] + 2)
            for b in range(2):
                nc.vector.tensor_tensor(v_sb[:, b, :], pair[1][:, b * T:(b + 1) * T], bv[:, :], ALU.add).then_inc(v_done, 1)
            ada_half(ADA_ATTN - 1, 1)
            rest_up(U0[ATTN] + 4, 0)
            rest_down(D0[ATTN] + 1, 1)
            rotate(1, col("q_gain"), q_rot[:, 0, :])
            rest_up(U0[ATTN] + 5, 1)
            for r in range(GROUP):
                softmax_columns(r)
                if r < GROUP - 1:
                    rotate(r + 2, col("q_gain"), q_rot[:, (r + 1) % 2, :])
                if r < 2:
                    ada_half(ADA_ATTN, r)
                if r in (1, 2):
                    rest_up(U0[ATTN] + r + 5, (r + 5) % 2)
                if r:
                    rest_outputs(r - 1)
                normalise(r)
                if r == 2:
                    gate_column(ATTN)
                    column(nc.vector.tensor_tensor(gb_col[:, :], mod_cols(0, 5), col("b_o"), ALU.mult))
                    for j in range(KC):
                        ins = nc.vector.tensor_scalar(x[:, j, :], x[:, j, :], gb_col[:, j:j + 1], None, ALU.add)
                    column(ins)
            rest_outputs(GROUP - 1)
            prepare(FFN1, ADA_ATTN + 1)
            for t in range(KC - 1):
                rest_down(D0[ATTN] + t + 2, t % 2)
            add_output(ATTN)

            ffn(FFN1, then=(FFN2, 22))
            ffn(FFN2, rest_first=True, then=(CONV, ADA_OF[FFN3][0]))

            norm(CONV)
            rest_down(D0[CONV], 0)
            for i in range(KC // 2):
                def conv(s):
                    j = 2 * i + s
                    u = cv_u[:, s, :]
                    dve.wait_ge(cv_c, j + 1)
                    n = 10 * i + 5 * s
                    nc.vector.tensor_tensor(u[:, 2:2 + T], gate_s[:, s, :], pair[(3 * i + s) % 2][:, T:2 * T],
                                            ALU.mult).then_inc(cv_in, 1)
                    dve.wait_ge(cv_in, j + 1)
                    for w in range(3):
                        tap = col("conv_w", w * KC + j, 1)
                        if w == 0:
                            nc.vector.tensor_scalar(prod[:, s, :], u[:, 0:T], tap, None, ALU.mult).then_inc(cv_step, 1)
                        else:
                            dve.wait_ge(cv_step, n0[0])
                            nc.vector.scalar_tensor_tensor(out=prod[:, s, :], in0=u[:, w:w + T], scalar=tap,
                                                           in1=prod[:, s, :], op0=ALU.mult, op1=ALU.add).then_inc(cv_step, 1)
                        n0[0] += 1
                n0 = [10 * i]
                conv(0)
                rest_up(U0[CONV] + 3 * i + 2, (3 * i + 2) % 2)
                if i:
                    rest_down(D0[CONV] + 2 * i - 1, 1)
                conv(1)
                if i < KC // 2 - 1:
                    rest_up(U0[CONV] + 3 * i + 3, (3 * i + 3) % 2)
                dve.wait_ge(up_done, U0[CONV] + 3 * i + 3)
                dve.wait_ge(cv_step, n0[0])
                for s in range(2):
                    nc.vector.tensor_tensor(cv_y[:, s, :], prod[:, s, :], pair[(3 * i + 2) % 2][:, s * T:(s + 1) * T],
                                            ALU.mult).then_inc(cv_step, 2)
                    n0[0] += 2
                for s in range(2):
                    dve.wait_ge(ah_done, AH0[CONV] + 2 * i + s + 1)
                    nc.vector.tensor_tensor(o_lo[:, 2 * i + s, :], cv_y[:, s, :], o_hi[:, 2 * i + s, :].bitcast(F32),
                                            ALU.subtract).then_inc(al_done, 1)
                if i < KC // 2 - 1:
                    rest_up(U0[CONV] + 3 * i + 4, (3 * i + 4) % 2)
                if i:
                    rest_down(D0[CONV] + 2 * i, 0)
            rest_down(D0[CONV] + KC - 1, 1)
            gate_column(CONV)
            prepare(FFN3, ADA_UNITS)
            rest_up(U0[FFN3], 0)
            add_output(CONV)
            rest_up(U0[FFN3] + 1, 1)
            ffn(FFN3, rest_first=True)

        @block.gpsimd
        def _(pool):
            pool.wait_ge(h_done, (ATTN + 1) * KC)
            nc.gpsimd.memset(k_rot[:, :, :], 0.0).then_inc(k_zero, 1)

        @block.tensor
        def _(pe):
            SQUARES_FROM = 5

            def three(out, w_hi, w_lo, m_hi, m_lo, start, stop):
                nc.tensor.matmul(out, w_hi, m_hi, start=start, stop=False, skip_group_check=True)
                nc.tensor.matmul(out, w_hi, m_lo, start=False, stop=False, skip_group_check=True)
                return nc.tensor.matmul(out, w_lo, m_hi, start=False, stop=stop, skip_group_check=True)

            def up(ph, f, s, first=False):
                pe.wait_ge(up_lo_done, U0[ph] + f + 1)
                for k in range(KC):
                    if first:
                        pe.wait_ge(hh_done, ph * KC + k + 1)
                        for c in range(2):
                            at = (2 * k + c) * P
                            for w in (up_hi, up_lo):
                                nc.tensor.matmul(pair[s][:, c * T:(c + 1) * T], w[:, s, at:at + P], h_hi[:, k, :],
                                                 start=k == 0 and c == 0 and w is up_hi, stop=False,
                                                 skip_group_check=True)
                        pe.wait_ge(h_done, ph * KC + k + 1)
                    for c in range(2):
                        at = (2 * k + c) * P
                        if first:
                            ins = nc.tensor.matmul(pair[s][:, c * T:(c + 1) * T], up_hi[:, s, at:at + P], h_lo[:, k, :],
                                                   start=False, stop=k == KC - 1, skip_group_check=True)
                            continue
                        ins = three(pair[s][:, c * T:(c + 1) * T], up_hi[:, s, at:at + P], up_lo[:, s, at:at + P],
                                    h_hi[:, k, :], h_lo[:, k, :], k == 0 and c == 0, k == KC - 1)
                ins.then_inc(up_done, 1)

            def square_sum(ph, j):
                pe.wait_ge(sq_done, ph * KC + j + 1)
                ins = nc.tensor.matmul(stat[:, 0:T], mean_w[:, :], sq[:, j, :], start=j == 0, stop=j == KC - 1)
                if j == KC - 1:
                    ins.then_inc(mean_done, 1)

            def down(n, s, m_hi, m_lo, first=False, last=False, then=None):
                pe.wait_ge(dn_lo_done, n + 1)
                for j in range(KC):
                    ins = three(acc[j // 2][:, (j % 2) * T:(j % 2 + 1) * T], dn_hi[:, s, j * P:(j + 1) * P],
                                dn_lo[:, s, j * P:(j + 1) * P], m_hi, m_lo, first and j % 2 == 0, last)
                    if last and j % 2 and j < KC - 1:
                        ins.then_inc(bank_done, 1)
                    if last and j == KC - 1:
                        ins.then_inc(dn_done, 1)
                    if then is not None and j >= SQUARES_FROM:
                        square_sum(then, j - SQUARES_FROM)
                if not last:
                    ins.then_inc(dn_done, 1)
                if then is not None:
                    for j in range(KC - SQUARES_FROM, KC):
                        square_sum(then, j)

            def ffn(ph, then=None):
                def up_f(f, s):
                    if not isinstance(f, int) or f >= 2:
                        pe.wait_ge(prod_done, FFN_NUMBER[ph] * NF + f - 1)
                    up(ph, f, s, isinstance(f, int) and f == 0)

                def down_f(f, s, **kw):
                    pe.wait_ge(al_done, AH0[ph] + f + 1)
                    down(D0[ph] + f, s, a_hi[:, s, :], a_lo[:, s, :], **kw)

                up_f(0, 0)
                up_f(1, 1)
                down_f(0, 0, first=True)
                with pe.Fori(1, NF // 2 - 1) as i:
                    up_f(2 * i, 0)
                    down_f(2 * i - 1, 1)
                    up_f(2 * i + 1, 1)
                    down_f(2 * i, 0)
                up_f(NF - 2, 0)
                down_f(NF - 3, 1)
                up_f(NF - 1, 1)
                down_f(NF - 2, 0)
                down_f(NF - 1, 1, last=True, then=then)

            pe.wait_ge(mean_w_in, 16)
            for j in range(KC):
                square_sum(FFN0, j)
            ffn(FFN0, then=ATTN)
            pe.wait_ge(consts_in, 16 * N_CONST_DMAS)

            def head_norm(n):
                pe.wait_ge(squared, n + 1)
                if n:
                    pe.wait_ge(head_rstd, 2 * n - 1)
                for t in range(2):
                    ins = nc.tensor.matmul(stat[:, 0:T], head_w[:, :], qk_sq[:, t * T:(t + 1) * T],
                                           start=t == 0, stop=t == 1)
                ins.then_inc(head_mean, 1)

            def scores(r):
                pe.wait_ge(rot_done, r + 2)
                q = q_rot[:, r % 2, :]
                for g in range(KV):
                    if KV * r + g >= 2:
                        pe.wait_ge(masked, KV * r + g - 1)
                    for b in range(2):
                        out = acc[g % 2][:, b * P:S_COLS if b else P]
                        for t in range(2):
                            ins = nc.tensor.matmul(out, q[:, t * T + b * P:t * T + (b + 1) * P],
                                                   k_rot[:, t * KV + g, 0:(b + 1) * P],
                                                   start=t == 0, stop=t == 1)
                    ins.then_inc(scored, 1)

            def turn(r, g):
                n = KV * r + g
                pe.wait_ge(norm_done, 2 * n + 2)
                if n >= 2:
                    pe.wait_ge(pt_done, n - 1)
                for c in range(3):
                    ins = nc.tensor.transpose(acc[2 + g % 2][:, c * P:(c + 1) * P],
                                              probs[:, r % 2, g, c * P:(c + 1) * P], ident[:, :])
                ins.then_inc(pt_ready, 1)

            def weigh(r, g):
                n = KV * r + g
                pe.wait_ge(pt_done, n + 1)
                if n == 0:
                    pe.wait_ge(v_done, 2)
                t = n // 2
                if g % 2 == 0 and t >= 2:
                    pe.wait_ge(ol_done, t - 1)
                rows = slice((g % 2) * HD, (g % 2 + 1) * HD)
                for b, c, start, stop in ((0, 0, True, True), (0, 1, True, False), (1, 2, False, True)):
                    q = 0 if c == 0 else P
                    ins = nc.tensor.matmul(o_bank[t % 2][rows, q:q + P], v_sb[:, b, g * HD:(g + 1) * HD],
                                           p_t[:, g % 2, c * P:(c + 1) * P], start=start, stop=stop)
                ins.then_inc(pv_done, 1)

            def heads(r):
                turn(r, 0)
                for g in range(KV):
                    if g + 1 < KV:
                        turn(r, g + 1)
                    weigh(r, g)

            up(ATTN, 0, 0, True)
            pe.wait_ge(up_lo_done, U0[ATTN] + 2)
            for b in range(2):
                for k in range(KC):
                    at = 2 * k * P
                    blk = slice(b * P, (b + 1) * P)
                    out = pair[1][:, b * T:(b + 1) * T]
                    nc.tensor.matmul(out, h_hi[:, k, blk], up_hi[:, 1, at:at + T], start=k == 0, stop=False,
                                     skip_group_check=True)
                    nc.tensor.matmul(out, h_lo[:, k, blk], up_hi[:, 1, at:at + T], start=False, stop=False,
                                     skip_group_check=True)
                    ins = nc.tensor.matmul(out, h_hi[:, k, blk], up_lo[:, 1, at:at + T], start=False, stop=k == KC - 1,
                                           skip_group_check=True)
                if b == 0:
                    head_norm(0)
            ins.then_inc(up_done, 1)
            pe.wait_ge(biased, 2)
            up(ATTN, 2, 0)
            pe.wait_ge(v_done, 2)
            up(ATTN, 3, 1)
            head_norm(1)
            pe.wait_ge(biased, 4)
            up(ATTN, 4, 0)
            for r in range(GROUP):
                scores(r)
                if r < GROUP - 1:
                    head_norm(r + 2)
                if r == 0:
                    pe.wait_ge(biased, 6)
                    up(ATTN, 5, 1)
                else:
                    heads(r - 1)
            heads(GROUP - 1)
            pe.wait_ge(masked, KV * GROUP)
            pe.wait_ge(pt_done, KV * GROUP)
            for t in range(KC):
                pe.wait_ge(ol_done, t + 1)
                down(D0[ATTN] + t, t % 2, o_hi[:, t, :], o_lo[:, t, :], first=t == 0, last=t == KC - 1,
                     then=FFN1 if t == KC - 1 else None)

            ffn(FFN1, then=FFN2)
            ffn(FFN2, then=CONV)

            def down_pair(i):
                for s in range(2):
                    t = 2 * i + s
                    pe.wait_ge(al_done, AH0[CONV] + t + 1)
                    down(D0[CONV] + t, s, o_hi[:, t, :], o_lo[:, t, :], first=t == 0, last=t == KC - 1,
                         then=FFN3 if t == KC - 1 else None)
            for i in range(KC // 2):
                for s in range(3):
                    u = 3 * i + s
                    if u >= 2:
                        v = u - 2
                        if v % 3 == 2:
                            pe.wait_ge(cv_step, 10 * (v // 3) + 10)
                        else:
                            pe.wait_ge(cv_in, 2 * (v // 3) + v % 3 + 1)
                    up(CONV, u, u % 2, u == 0)
                if i:
                    down_pair(i - 1)
            down_pair(KC // 2 - 1)
            ffn(FFN3)


AH0 = {FFN0: 0, FFN1: NF, FFN2: 2 * NF, CONV: 3 * NF, FFN3: 3 * NF + KC}


def kernel(x, c, positions, norm_gain, w_ada, b_ada, w_ffn_up, w_ffn_down, attn_w_qkv, attn_b_qkv,
           attn_q_gain, attn_k_gain, attn_sinks, attn_w_o, attn_b_o, conv_w_in, conv_w, conv_w_out):
    import concourse.bacc as bacc
    from concourse.bass_utils import run_bass_kernel_spmd as run

    f32 = np.float32

    def chunks(v):
        return np.asarray(v).reshape(-1, KC, P).transpose(2, 0, 1).reshape(P, -1)

    bq = np.asarray(attn_b_qkv)[0, :HEADS * HD].reshape(KV, GROUP, 2, HALF)
    bk = np.asarray(attn_b_qkv)[0, HEADS * HD:(HEADS + KV) * HD].reshape(KV, 2, HALF)
    v_at = (HEADS + KV) * HD

    def per_half(g):
        return np.broadcast_to(np.asarray(g)[0].reshape(1, 2, HALF).transpose(0, 2, 1), (KV, HALF, 2)).reshape(P, 2)

    sinks = np.asarray(attn_sinks)[0].reshape(KV, GROUP).transpose(1, 0)
    sinks = np.broadcast_to(sinks[None, :, None, :], (P, GROUP, 2, KV)).reshape(P, -1)
    inv = (f32(10000.0) ** (-np.arange(0, HD, 2, dtype=f32) / f32(HD))).astype(f32)
    parts = {
        "gain": chunks(norm_gain), "b_ada": chunks(b_ada), "conv_w": chunks(conv_w), "b_o": chunks(attn_b_o),
        "b_q": bq.transpose(0, 3, 1, 2).reshape(P, -1), "b_k": bk.transpose(0, 2, 1).reshape(P, -1),
        "q_gain": per_half(attn_q_gain), "k_gain": per_half(attn_k_gain), "sinks": sinks,
        "inv_freq": np.tile(inv, KV)[:, None], "half_pi": np.full((P, 1), math.pi / 2, f32),
        "eps": np.full((P, 1), EPS, f32),
    }
    cols = np.concatenate([parts[n] for n in COLS], axis=1)
    q = np.arange(P)[:, None]
    mask = np.zeros((P, S_COLS), f32)
    mask[:, :P][q < np.arange(P)[None]] = MASKED
    rel = P + q - np.arange(2 * P)[None]
    mask[:, P:][(rel < 0) | (rel >= P)] = MASKED
    w_qkv = np.asarray(attn_w_qkv)[0].reshape(KC, P, -1)
    wq = w_qkv[:, :, :HEADS * HD].reshape(KC, P, KV, GROUP, 2, HALF).transpose(3, 1, 0, 4, 2, 5).reshape(GROUP, P, UP)
    wk = w_qkv[:, :, HEADS * HD:v_at].reshape(KC, P, KV, 2, HALF).transpose(1, 0, 3, 2, 4).reshape(1, P, UP)
    wv = w_qkv[:, :, v_at:].transpose(1, 0, 2).reshape(1, P, UP)
    w_in = np.asarray(conv_w_in)[0].reshape(KC, P, 3, KC // 2, 2, P)
    cv = w_in[:, :, 1:].transpose(3, 4, 1, 0, 2, 5).reshape(KC // 2, 2, P, UP)
    gb = w_in[:, :, 0].transpose(2, 1, 0, 3, 4).reshape(KC // 2, 1, P, UP)
    arrays = {
        "x_t": np.asarray(x)[0].T,
        "c_d": np.asarray(c)[0],
        "cols_d": cols,
        "pos_d": np.asarray(positions)[0],
        "bv_d": np.asarray(attn_b_qkv)[0, v_at:],
        "ident_d": np.eye(P, dtype=f32),
        "ones_d": np.full((P, P), 1 / D, f32),
        "heads_d": np.kron(np.eye(KV, dtype=f32), np.full((HALF, HALF), 1 / HD, f32)),
        "mask_d": mask,
        "w_ada_d": np.asarray(w_ada).reshape(2, D, -1, AH, P).transpose(0, 2, 4, 3, 1).reshape(-1, P, AH * D),
        "w_up_d": np.asarray(w_ffn_up).reshape(4, KC, P, 2, NF, P).transpose(0, 4, 2, 1, 3, 5).reshape(-1, P, UP),
        "w_down_d": np.asarray(w_ffn_down).reshape(-1, P, DN),
        "w_qkv_d": np.concatenate([wk, wv, wq]),
        "w_o_d": np.asarray(attn_w_o)[0].reshape(2, 2, GROUP, HD, D).transpose(2, 0, 1, 3, 4).reshape(KC, P, D),
        "w_cin_d": np.concatenate([cv, gb], axis=1).reshape(-1, P, UP),
        "w_cout_d": np.asarray(conv_w_out)[0].reshape(KC, P, D),
    }
    arrays = {n: np.ascontiguousarray(a) for n, a in arrays.items()}
    nc = bacc.Bacc("TRN2", target_bir_lowering=False, num_devices=1)
    aps = [nc.dram_tensor(n, a.shape, mybir.dt.from_np(a.dtype), kind="ExternalInput").ap() for n, a in arrays.items()]
    aps.append(nc.dram_tensor("out_t", (D, T), F32, kind="ExternalOutput").ap())
    build(nc, *aps)
    r = run(nc, [arrays], core_ids=[0])
    return r.results[0]["out_t"].T.reshape(1, T, D)
```

```python
from contextlib import ExitStack
import math

import numpy as np

import concourse.bass as bass
from concourse import mybir
from concourse.alu_op_type import AluOpType as ALU

F32 = mybir.dt.float32
F32R = mybir.dt.float32r
I32 = mybir.dt.int32
ACT = mybir.ActivationFunctionType
AX = mybir.AxisListType

P = 128
D = 1024
T = 256
KC = D // P
FF = 2816
NF = FF // P
HEADS, KV, HD = 16, 4, 64
GROUP = HEADS // KV
HALF = HD // 2
EPS = 1e-6
N_ADA = 9
UP = 2 * KC * P
DN = D
AC = 4
AH = AC // 2
ADA_UNITS = 2 * N_ADA * KC // AC
N_ADA_START = 2 * KC // AC
MASKED = -3.0e38

FFN0, ATTN, FFN1, FFN2, CONV, FFN3 = range(6)
UPS = [NF, 6, NF, NF, 12, NF]
DOWNS = [NF, KC, NF, NF, KC, NF]
U0 = [sum(UPS[:n]) for n in range(6)]
D0 = [sum(DOWNS[:n]) for n in range(6)]
N_UP, N_DOWN = sum(UPS), sum(DOWNS)
FFN_NUMBER = {FFN0: 0, FFN1: 1, FFN2: 2, FFN3: 3}
ADA_OF = {FFN0: (N_ADA_START, NF // 2)}
ADA_ATTN = N_ADA_START + NF // 2
ADA_OF[FFN1] = (ADA_ATTN + 1, (ADA_UNITS - ADA_ATTN - 1) // 2)
ADA_OF[FFN2] = (ADA_OF[FFN1][0] + ADA_OF[FFN1][1], ADA_UNITS - ADA_OF[FFN1][0] - ADA_OF[FFN1][1])
ADA_OF[FFN3] = (ADA_UNITS, 0)


def ada_beside(ph, i):
    first, count = ADA_OF[ph]
    if count == 0:
        return [None, None]
    if ph in (FFN1, FFN2):
        halves = [(first + i - 1, 1), (first + i, 0)]
    else:
        halves = [(first + i, 0), (first + i, 1)]
    return [None if isinstance(i, int) and not first <= n < first + count else (n, s) for n, s in halves]


COLS = {}
_at = 0
for _name, _n in (("gain", 6 * KC), ("b_ada", 2 * N_ADA * KC), ("conv_w", 3 * KC), ("b_o", KC),
                  ("b_q", 2 * GROUP), ("b_k", 2), ("q_gain", 2), ("k_gain", 2), ("sinks", GROUP * 2 * KV),
                  ("inv_freq", 1), ("half_pi", 1), ("eps", 1)):
    COLS[_name] = (_at, _at + _n)
    _at += _n
N_COLS = _at
S_COLS = 3 * P


def build(nc, x_t, c_d, cols_d, pos_d, bv_d, ident_d, ones_d, heads_d, mask_d, w_ada, w_up, w_down, w_qkv, w_o,
          w_cin, w_cout, out_t):
    up_of = [w_up, w_qkv, w_up, w_up, w_cin, w_up]
    down_of = [w_down, w_o, w_down, w_down, w_cout, w_down]

    def first_row(ph):
        return FFN_NUMBER[ph] * NF if ph in FFN_NUMBER else 0

    with ExitStack() as ctx:
        def sb(name, shape, dt=F32):
            return ctx.enter_context(nc.sbuf_tensor(name, shape, dt))

        def sem(name):
            return ctx.enter_context(nc.semaphore(name))

        up_raw = sb("up_raw", [P, 2, UP])
        up_hi = sb("up_hi", [P, 2, UP], F32R)
        up_lo = sb("up_lo", [P, 2, UP], F32R)
        dn_raw = sb("dn_raw", [P, 2, DN])
        dn_hi = sb("dn_hi", [P, 2, DN], F32R)
        dn_lo = sb("dn_lo", [P, 2, DN], F32R)
        ada_raw = sb("ada_raw", [P, 2, AH * D])
        ada_out = sb("ada_out", [P, 4 * AH])
        mod = sb("mod", [P, 2 * N_ADA * KC])
        cols = sb("cols", [P, N_COLS])
        c_row = sb("c_row", [P, D])
        ident = sb("ident", [P, P])
        mean_w = sb("mean_w", [P, P])
        head_w = sb("head_w", [P, P])
        mask = sb("mask", [P, S_COLS])
        pos = sb("pos", [P, T], I32)
        bv = sb("bv", [P, KV * HD])
        cos2 = sb("cos2", [P, 2 * T])
        sin2 = sb("sin2", [P, 2 * T])
        x = sb("x", [P, KC, T])
        sq = sb("sq", [P, KC, T])
        xs = sb("xs", [P, KC, T])
        h_hi = sb("h_hi", [P, KC, T], F32R)
        h_lo = sb("h_lo", [P, KC, T], F32R)
        ln_ms = sb("ln_ms", [P, T])
        rstd = sb("rstd", [P, T])
        a_col = sb("a_col", [P, KC])
        g_col = sb("g_col", [P, KC])
        gb_col = sb("gb_col", [P, KC])
        gate_s = sb("gate_s", [P, 2, T])
        prod = sb("prod", [P, 2, T])
        a_hi = sb("a_hi", [P, 2, T], F32R)
        a_lo = sb("a_lo", [P, 2, T], F32R)
        qk_t = sb("qk_t", [P, 2 * T])
        qk_sq = sb("qk_sq", [P, 2 * T])
        qk_n = sb("qk_n", [P, 2 * T])
        qk_c = sb("qk_c", [P, 2 * T])
        qk_s = sb("qk_s", [P, 2 * T])
        ang = qk_c[:, :].rearrange("p (a t) -> p a t", a=2)
        qk_r = sb("qk_r", [P, T])
        k_rot = xs
        q_rot = sb("q_rot", [P, 2, 2 * T])
        v_sb = sb("v_sb", [P, 2, KV * HD])
        probs = sb("probs", [P, 2, KV, S_COLS])
        m_col = sb("m_col", [P, 2, 2 * KV])
        nm_col = sb("nm_col", [P, 2, 2 * KV])
        sd_col = sb("sd_col", [P, 2, 2 * KV])
        es_col = sb("es_col", [P, 2, 2 * KV])
        su_col = sb("su_col", [P, 2, 2 * KV])
        de_col = sb("de_col", [P, 2, 2 * KV])
        ri_col = sb("ri_col", [P, 2, 2 * KV])
        p_t = sb("p_t", [P, 2, S_COLS])
        o_hi = sb("o_hi", [P, KC, T], F32R)
        o_lo = sb("o_lo", [P, KC, T], F32R)
        cv_u = sb("cv_u", [P, 2, 2 + T])
        cv_y = sb("cv_y", [P, 2, T])

        acc = [ctx.enter_context(nc.psum_tensor(f"acc{n}", [P, 2 * T], F32)) for n in range(4)]
        pair = [ctx.enter_context(nc.psum_tensor(f"pair{n}", [P, 2 * T], F32)) for n in range(2)]
        stat = ctx.enter_context(nc.psum_tensor("stat", [P, 2 * T], F32))
        aux = ctx.enter_context(nc.psum_tensor("aux", [P, 2 * T], F32))

        o_bank = (aux, pair[0])

        def dn_slot(n, s):
            if isinstance(n, int) and D0[ATTN] <= n < D0[FFN1] and (n - D0[ATTN]) % 4 >= 2:
                return sq[:, :, :].rearrange("p k t -> p (k t)")[:, s * DN:(s + 1) * DN]
            return dn_raw[:, s, :]

        def s_bank(r, g):
            return (acc[0], acc[1], aux if r < 2 else pair[1], acc[0])[g]

        consts_in = sem("consts_in")
        x_in = sem("x_in")
        up_in = [sem(f"up_in{n}") for n in range(2)]
        dn_in = [sem(f"dn_in{n}") for n in range(2)]
        ada_in = [sem(f"ada_in{n}") for n in range(2)]
        c_in, cols_in, pos_in, mean_w_in = sem("c_in"), sem("cols_in"), sem("pos_in"), sem("mean_w_in")
        start_in = [sem(f"start_in{n}") for n in range(2)]
        stored = sem("stored")
        up_hi_done, up_lo_done = sem("up_hi_done"), sem("up_lo_done")
        dn_hi_done, dn_lo_done = sem("dn_hi_done"), sem("dn_lo_done")
        up_done, dn_done = sem("up_done"), sem("dn_done")
        bank_done = sem("bank_done")
        c_done = sem("c_done")
        ada_step = sem("ada_step")
        mod_done = sem("mod_done")
        x_done, sq_done, mean_done, rstd_done = sem("x_done"), sem("sq_done"), sem("mean_done"), sem("rstd_done")
        ln_done, xs_done, hh_done, h_done = sem("ln_done"), sem("xs_done"), sem("hh_done"), sem("h_done")
        col_step = sem("col_step")
        gate_done, prod_done, ah_done, al_done = sem("gate_done"), sem("prod_done"), sem("ah_done"), sem("al_done")
        tab_step, tab_done = sem("tab_step"), sem("tab_done")
        biased, squared, head_mean, head_rstd, rope_step, rot_done = (sem(n) for n in (
            "biased", "squared", "head_mean", "head_rstd", "rope_step", "rot_done"))
        v_done, scored, masked, soft_step, exp_done, norm_done = (sem(n) for n in (
            "v_done", "scored", "masked", "soft_step", "exp_done", "norm_done"))
        pt_ready, pt_done, pv_done, oh_done, ol_done = (sem(n) for n in (
            "pt_ready", "pt_done", "pv_done", "oh_done", "ol_done"))
        k_zero = sem("k_zero")
        cv_c, cv_in, cv_step, cv_pad = sem("cv_c"), sem("cv_in"), sem("cv_step"), sem("cv_pad")

        def col(name, a=0, n=None):
            lo, hi = COLS[name]
            return cols[:, lo + a:hi if n is None else lo + a + n]

        def mod_cols(layer, v):
            at = (layer * N_ADA + v) * KC
            return mod[:, at:at + KC]

        N_CONST_DMAS = 4
        SOFT = 2 * KV + 3
        start_slots = [(ada_raw[:, 0, :], ada_in[0]), (ada_raw[:, 1, :], ada_in[1]),
                       (dn_raw[:, :, :].rearrange("p k t -> p (k t)"), start_in[0]),
                       (probs[:, :, :, :].rearrange("p a g n -> p (a g n)")[:, 0:AH * D], start_in[1])]
        start_halves = list(range(N_ADA_START, 2 * N_ADA_START)) + list(range(N_ADA_START))
        norm_of = {FFN0: (0, 0), ATTN: (0, 1), FFN1: (0, 2), FFN2: (1, 0), CONV: (1, 1), FFN3: (1, 2)}

        block = ctx.enter_context(nc.Block())

        @block.sync
        def _(sp):
            def load_up(ph, f, s):
                n = U0[ph] + f
                if not isinstance(n, int) or n >= 2:
                    sp.wait_ge(up_lo_done, n - 1)
                sp.dma_start(up_raw[:, s, :],
                             up_of[ph][bass.ds(first_row(ph) + f, 1), :, :].rearrange("a p n -> p (a n)")
                             ).then_inc(up_in[s], 16)

            def load_down(ph, f, s):
                n = D0[ph] + f
                if ph == ATTN and f >= 2:
                    if f < 4:
                        sp.wait_ge(mean_done, ATTN + 1)
                    else:
                        sp.wait_ge(dn_lo_done, n - 3)
                    sp.wait_ge(dn_in[s], 8 * (n - s))
                elif not isinstance(n, int) or n >= 2:
                    sp.wait_ge(dn_lo_done, n - 1)
                sp.dma_start(dn_slot(n, s),
                             down_of[ph][bass.ds(first_row(ph) + f, 1), :, :].rearrange("a p n -> p (a n)")
                             ).then_inc(dn_in[s], 16)

            def load_start(i):
                slot, landed = start_slots[i % 4]
                if i >= 4:
                    sp.wait_ge(ada_step, AH * (i - 3))
                sp.dma_start(slot, w_ada[start_halves[i], :, :]).then_inc(landed, 16)

            sp.dma_start(cols[:, :], cols_d).then_inc(cols_in, 16)
            sp.dma_start(pos[:, :], pos_d.partition_broadcast(P)).then_inc(pos_in, 16)
            sp.dma_start(c_row[:, :], c_d.partition_broadcast(P)).then_inc(c_in, 16)
            for i in (0, 1):
                load_start(i)
            sp.dma_start(x[:, :, :], x_t.rearrange("(k p) t -> p k t", p=P)).then_inc(x_in, 16)
            sp.dma_start(mean_w[:, :], ones_d).then_inc(mean_w_in, 16)
            for i in (2, 3, 4, 5):
                load_start(i)
            load_up(FFN0, 0, 0)
            for i in (6, 7):
                load_start(i)
            load_up(FFN0, 1, 1)
            sp.wait_ge(ada_step, AH * 7)
            load_down(FFN0, 0, 0)

            def ffn_loads(ph, ups_there=False):
                if not ups_there:
                    load_up(ph, 0, 0)
                    load_up(ph, 1, 1)
                if ph != FFN0:
                    load_down(ph, 0, 0)
                with sp.Fori(1, NF // 2) as i:
                    load_up(ph, 2 * i, 0)
                    load_down(ph, 2 * i - 1, 1)
                    load_up(ph, 2 * i + 1, 1)
                    load_down(ph, 2 * i, 0)
                load_down(ph, NF - 1, 1)

            ffn_loads(FFN0, ups_there=True)
            sp.dma_start(bv[:, :], bv_d.partition_broadcast(P)).then_inc(consts_in, 16)
            sp.dma_start(ident[:, :], ident_d).then_inc(consts_in, 16)
            sp.dma_start(head_w[:, :], heads_d).then_inc(consts_in, 16)
            sp.dma_start(mask[:, :], mask_d).then_inc(consts_in, 16)
            for kind, n in (("u", 0), ("d", 0), ("u", 1), ("u", 2), ("u", 3), ("d", 1), ("d", 2), ("d", 3), ("u", 4),
                            ("u", 5), ("next", 0), ("next", 1), ("d", 4), ("d", 5), ("d", 6), ("d", 7)):
                if kind == "next":
                    load_up(FFN1, n, n)
                else:
                    (load_up if kind == "u" else load_down)(ATTN, n, n % 2)
            ffn_loads(FFN1, ups_there=True)
            ffn_loads(FFN2)
            for i in range(4):
                load_up(CONV, 3 * i, (3 * i) % 2)
                if i:
                    load_down(CONV, 2 * i - 1, 1)
                load_up(CONV, 3 * i + 1, (3 * i + 1) % 2)
                load_up(CONV, 3 * i + 2, (3 * i + 2) % 2)
                load_down(CONV, 2 * i, 0)
            load_down(CONV, KC - 1, 1)
            ffn_loads(FFN3)
            for j in range(KC):
                sp.wait_ge(x_done, 6 * KC + j + 1 - KC)
                sp.dma_start(out_t[j * P:(j + 1) * P, :], x[:, j, :]).then_inc(stored, 16)
            sp.wait_ge(stored, 16 * KC)

        @block.scalar
        def _(act):
            def round_up(n, s):
                if isinstance(n, int) and n >= N_UP:
                    return
                act.wait_ge(up_in[s], 8 * (n - s) + 16)
                if not isinstance(n, int) or n >= 2:
                    act.wait_ge(up_done, n - 1)
                nc.scalar.activation(up_hi[:, s, :], up_raw[:, s, :], ACT.Copy).then_inc(up_hi_done, 1)

            def round_down(n, s):
                if isinstance(n, int) and n >= N_DOWN:
                    return
                act.wait_ge(dn_in[s], 8 * (n - s) + 16)
                if not isinstance(n, int) or n >= 2:
                    act.wait_ge(dn_done, n - 1)
                nc.scalar.activation(dn_hi[:, s, :], dn_slot(n, s), ACT.Copy).then_inc(dn_hi_done, 1)

            def load_half(n, s):
                if isinstance(n, int) and n >= ADA_UNITS:
                    return
                if isinstance(n, int) and n == N_ADA_START:
                    act.wait_ge(ada_step, AH * (5 + s))
                else:
                    act.wait_ge(ada_step, AC * (n - 1) + AH * (s + 1))
                act.dma_start(ada_raw[:, s, :],
                              w_ada[bass.ds(2 * n + s, 1), :, :].rearrange("a p n -> p (a n)")
                              ).then_inc(ada_in[s], 16)

            def norm_table():
                nc.scalar.preload_act_table_set("natural_log_exp_and_others")

            def squares(ph):
                if ph in (FFN0, FFN3):
                    norm_table()
                for j in range(KC):
                    if ph == FFN0:
                        if j == 0:
                            act.wait_ge(x_in, 16)
                    else:
                        act.wait_ge(x_done, (ph - 1) * KC + j + 1)
                    nc.scalar.activation(sq[:, j, :], x[:, j, :], ACT.Square).then_inc(sq_done, 1)

            def scale(ph):
                act.wait_ge(mean_done, ph + 1)
                nc.scalar.activation(ln_ms[:, :], stat[:, 0:T], ACT.Ln, bias=col("eps")).then_inc(ln_done, 1)
                act.wait_ge(ln_done, ph + 1)
                nc.scalar.activation(rstd[:, :], ln_ms[:, :], ACT.Exp, scale=-0.5).then_inc(rstd_done, 1)

            def shifted(ph):
                layer, sub = norm_of[ph]
                shift = mod_cols(layer, 3 * sub)
                for j in range(KC):
                    act.wait_ge(xs_done, ph * KC + j + 1)
                    if ph == FFN0:
                        if j == KC - AH:
                            round_up(1, 1)
                            load_half(N_ADA_START, 0)
                        act.wait_ge(mod_done, KC + j + 1)
                    nc.scalar.activation(h_hi[:, j, :], xs[:, j, :], ACT.Identity,
                                         bias=shift[:, j:j + 1]).then_inc(hh_done, 1)
                if ph in FFN_NUMBER:
                    nc.scalar.preload_act_table(ACT.Silu)

            def norm(ph):
                squares(ph)
                round_down(D0[ph], 0)
                scale(ph)
                shifted(ph)

            def hidden(ph, f, s, last=False):
                g = FFN_NUMBER[ph] * NF + f
                act.wait_ge(up_done, U0[ph] + f + 1)
                nc.scalar.activation(gate_s[:, s, :], pair[s][:, 0:T], ACT.Silu).then_inc(gate_done, 1)
                if last and ph != FFN3:
                    norm_table()
                if not isinstance(f, int) or f >= 2:
                    act.wait_ge(dn_done, D0[ph] + f - 1)
                act.wait_ge(prod_done, g + 1)
                nc.scalar.activation(a_hi[:, s, :], prod[:, s, :], ACT.Copy).then_inc(ah_done, 1)

            def ffn(ph):
                first, count = ADA_OF[ph]

                def period(f, s, ada):
                    hidden(ph, f, s)
                    round_up(U0[ph] + f + 2, s)
                    round_down(D0[ph] + f + 1, 1 - s)
                    if ada is not None:
                        load_half(ada[0] + 1, ada[1])

                def pair_of_periods(i):
                    even, odd = ada_beside(ph, i)
                    period(2 * i, 0, even)
                    period(2 * i + 1, 1, odd)
                last = NF // 2 - 1
                if ph != FFN0:
                    norm(ph)
                stop = min(last, count - 1) if count else last
                pair_of_periods(0)
                with act.Fori(1, stop) as i:
                    pair_of_periods(i)
                for i in range(stop, last):
                    pair_of_periods(i)
                period(NF - 2, 0, ada_beside(ph, last)[0])
                hidden(ph, NF - 1, 1, last=True)
                round_up(U0[ph] + NF + 1, 1)

            act.wait_ge(c_in, 16)
            nc.scalar.activation(c_row[:, :], c_row[:, :], ACT.Silu).then_inc(c_done, 1)
            act.wait_ge(cols_in, 16)
            act.wait_ge(tab_step, 8)
            for t in range(2):
                nc.scalar.activation(sin2[:, t * T:(t + 1) * T], ang[:, 0, :], ACT.Sin).then_inc(tab_done, 1)
                nc.scalar.activation(cos2[:, t * T:(t + 1) * T], ang[:, 1, :], ACT.Sin, scale=-1.0,
                                     bias=col("half_pi")).then_inc(tab_done, 1)
            squares(FFN0)
            scale(FFN0)
            round_up(0, 0)
            shifted(FFN0)
            round_down(0, 0)
            load_half(N_ADA_START, 1)
            ffn(FFN0)

            def bias_square(n, b):
                act.wait_ge(up_done, U0[ATTN] + (1 if n == 0 else n + 2))
                if n >= 1:
                    act.wait_ge(rope_step, 5 * n - 3)
                for t in range(2):
                    projected = pair[(0 if n == 0 else n + 1) % 2][:, t * T:(t + 1) * T]
                    nc.scalar.activation(qk_t[:, t * T:(t + 1) * T], projected, ACT.Identity,
                                         bias=b[:, t:t + 1]).then_inc(biased, 1)
                act.wait_ge(biased, 2 * n + 2)
                nc.scalar.activation(qk_sq[:, :], qk_t[:, :], ACT.Square).then_inc(squared, 1)

            def head_scale(n):
                act.wait_ge(head_mean, n + 1)
                nc.scalar.activation(qk_r[:, :], stat[:, 0:T], ACT.Ln, bias=col("eps")).then_inc(head_rstd, 1)
                act.wait_ge(head_rstd, 2 * n + 1)
                nc.scalar.activation(qk_r[:, :], qk_r[:, :], ACT.Exp, scale=-0.5).then_inc(head_rstd, 1)

            def exps(r, g):
                s = r % 2
                if g == 0:
                    act.wait_ge(soft_step, SOFT * (r + 1))
                    nc.scalar.activation(es_col[:, s, :], sd_col[:, s, :], ACT.Exp).then_inc(exp_done, 1)
                for b in range(2):
                    e = probs[:, s, g, 0:P] if b == 0 else probs[:, s, g, P:S_COLS]
                    nc.scalar.activation(e, e, ACT.Exp, bias=nm_col[:, s, b * KV + g:b * KV + g + 1],
                                         accum_out=su_col[:, s, b * KV + g:b * KV + g + 1]).then_inc(exp_done, 1)

            def turned(r, g):
                n = KV * r + g
                act.wait_ge(pt_ready, n + 1)
                if n >= 2:
                    act.wait_ge(pv_done, n - 1)
                nc.scalar.activation(p_t[:, g % 2, :], acc[2 + g % 2][:, 0:S_COLS], ACT.Copy).then_inc(pt_done, 1)

            def output(t):
                act.wait_ge(pv_done, 2 * t + 2)
                nc.scalar.activation(o_hi[:, t, :], o_bank[t % 2][:, 0:T], ACT.Copy).then_inc(oh_done, 1)

            def attend(r, also=None):
                turned(r, 0)
                turned(r, 1)
                if r < GROUP - 2:
                    head_scale(r + 3)
                turned(r, 2)
                output(2 * r)
                if also:
                    also(0)
                turned(r, 3)
                if also:
                    also(1)
                output(2 * r + 1)
                if also:
                    also(2)
                    also(3)

            norm(ATTN)
            bias_square(0, col("b_k"))
            round_up(U0[ATTN] + 2, 0)
            head_scale(0)
            round_up(U0[ATTN] + 3, 1)
            round_down(D0[ATTN] + 1, 1)
            bias_square(1, col("b_q", 0, 2))
            round_up(U0[ATTN] + 4, 0)
            head_scale(1)
            round_up(U0[ATTN] + 5, 1)
            bias_square(2, col("b_q", 2, 2))
            for r in range(GROUP):
                if r == 0:
                    head_scale(2)
                if r:
                    attend(r - 1, lambda g: exps(r, g))
                else:
                    for g in range(KV):
                        exps(r, g)
                if r < GROUP - 2:
                    bias_square(r + 3, col("b_q", 2 * r + 4, 2))
                    round_up(U0[FFN1] + r, r)
                    if r == 0:
                        load_half(ADA_ATTN, 1)
            attend(GROUP - 1)
            for t in range(KC - 2):
                round_down(D0[ATTN] + t + 2, t % 2)
                if t in (3, 5):
                    load_half(ADA_ATTN + 1, t // 4)

            ffn(FFN1)
            ffn(FFN2)

            norm(CONV)
            for i in range(KC // 2):
                for s in range(2):
                    u = 3 * i + s
                    act.wait_ge(up_done, U0[CONV] + u + 1)
                    nc.scalar.activation(gate_s[:, s, :], pair[u % 2][:, 0:T], ACT.Copy).then_inc(cv_c, 1)
                    if i < KC // 2 - 1 or s == 0:
                        round_up(U0[CONV] + u + 2, u % 2)
                    else:
                        round_down(D0[CONV] + 2 * i, 0)
                    if s == 0 and i:
                        round_down(D0[CONV] + 2 * i - 1, 1)
                for s in range(2):
                    act.wait_ge(cv_step, 10 * i + 2 * s + 8)
                    nc.scalar.activation(o_hi[:, 2 * i + s, :], cv_y[:, s, :], ACT.Copy).then_inc(ah_done, 1)
                if i < KC // 2 - 1:
                    round_up(U0[CONV] + 3 * i + 4, (3 * i + 4) % 2)
                    if i:
                        round_down(D0[CONV] + 2 * i, 0)
            round_down(D0[CONV] + KC - 1, 1)
            for n in range(2):
                round_up(U0[FFN3] + n, n)
            ffn(FFN3)

        @block.vector
        def _(dve):
            def rest_up(n, s):
                if isinstance(n, int) and n >= N_UP:
                    return
                dve.wait_ge(up_hi_done, n + 1)
                nc.vector.tensor_tensor(up_lo[:, s, :], up_raw[:, s, :], up_hi[:, s, :].bitcast(F32),
                                        ALU.subtract).then_inc(up_lo_done, 1)

            def rest_down(n, s):
                if isinstance(n, int) and n >= N_DOWN:
                    return
                dve.wait_ge(dn_hi_done, n + 1)
                nc.vector.tensor_tensor(dn_lo[:, s, :], dn_slot(n, s), dn_hi[:, s, :].bitcast(F32),
                                        ALU.subtract).then_inc(dn_lo_done, 1)

            def ada_sum(slot, at, k, before, depth=2):
                if not isinstance(before, int) or before >= depth:
                    dve.wait_ge(mod_done, AH * (before - depth + 1))
                w = slot[:, k * D:(k + 1) * D]
                nc.vector.tensor_tensor_reduce(out=w, in0=w, in1=c_row[:, :], scale=1.0, scalar=0.0,
                                               op0=ALU.mult, op1=ALU.add,
                                               accum_out=ada_out[:, AH * at + k:AH * at + k + 1]).then_inc(ada_step, 1)

            def keep(at, chunk, done):
                dve.wait_ge(ada_step, AH * done)
                nc.vector.tensor_tensor(mod[:, bass.ds(chunk, AH)], ada_out[:, AH * at:AH * (at + 1)],
                                        cols[:, bass.ds(COLS["b_ada"][0] + chunk, AH)], ALU.add
                                        ).then_inc(mod_done, AH)

            def ada_chunk(n, s, k):
                if k == 0:
                    dve.wait_ge(ada_in[s], 16 * (n - 1))
                ada_sum(ada_raw[:, s, :], s, k, 2 * n + s)
                if k == AH - 1:
                    keep(s, AC * n + AH * s, 2 * n + s + 1)

            def ada_half(n, s):
                for k in range(AH):
                    ada_chunk(n, s, k)

            small = [0]

            def column(ins):
                ins.then_inc(col_step, 1)
                small[0] += 1
                dve.wait_ge(col_step, small[0])

            def scale_column(ph):
                layer, sub = norm_of[ph]
                column(nc.vector.scalar_tensor_tensor(
                    out=a_col[:, :], in0=mod_cols(layer, 3 * sub + 1), scalar=1.0,
                    in1=col("gain", (3 * layer + sub) * KC, KC), op0=ALU.add, op1=ALU.mult))

            def prepare(ph, units):
                dve.wait_ge(mod_done, AC * units)
                scale_column(ph)

            def gate_column(ph):
                layer, sub = norm_of[ph]
                dve.wait_ge(mod_done, (layer * N_ADA + 3 * sub + 3) * KC)
                column(nc.vector.tensor_scalar(g_col[:, :], mod_cols(layer, 3 * sub + 2),
                                               0.5 if ph in FFN_NUMBER else 1.0, None, ALU.mult))

            def add_output(ph):
                for j in range(KC):
                    if j % 2 == 0 and j < KC - 2:
                        dve.wait_ge(bank_done, 3 * ph + j // 2 + 1)
                    elif j == KC - 2:
                        dve.wait_ge(dn_done, D0[ph] + DOWNS[ph])
                    nc.vector.scalar_tensor_tensor(out=x[:, j, :], in0=acc[j // 2][:, (j % 2) * T:(j % 2 + 1) * T],
                                                   scalar=g_col[:, j:j + 1], in1=x[:, j, :],
                                                   op0=ALU.mult, op1=ALU.add).then_inc(x_done, 1)

            def scale_chunk(ph, j):
                nc.vector.scalar_tensor_tensor(out=xs[:, j, :], in0=x[:, j, :], scalar=a_col[:, j:j + 1],
                                               in1=rstd[:, :], op0=ALU.mult, op1=ALU.mult).then_inc(xs_done, 1)

            def scaled(ph):
                dve.wait_ge(rstd_done, ph + 1)
                for j in range(KC):
                    scale_chunk(ph, j)

            def shifted_rest(ph, j):
                layer, sub = norm_of[ph]
                if ph == FFN0:
                    dve.wait_ge(mod_done, KC + j + 1)
                dve.wait_ge(hh_done, ph * KC + j + 1)
                nc.vector.scalar_tensor_tensor(out=h_lo[:, j, :], in0=xs[:, j, :],
                                               scalar=mod_cols(layer, 3 * sub)[:, j:j + 1],
                                               in1=h_hi[:, j, :].bitcast(F32), op0=ALU.add,
                                               op1=ALU.subtract).then_inc(h_done, 1)

            def norm(ph):
                dve.wait_ge(rstd_done, ph + 1)
                for j in range(KC):
                    scale_chunk(ph, j)
                    if j:
                        shifted_rest(ph, j - 1)
                shifted_rest(ph, KC - 1)

            def hidden(ph, f, s):
                g = FFN_NUMBER[ph] * NF + f
                dve.wait_ge(gate_done, g + 1)
                nc.vector.tensor_tensor(prod[:, s, :], gate_s[:, s, :], pair[s][:, T:2 * T],
                                        ALU.mult).then_inc(prod_done, 1)
                dve.wait_ge(ah_done, AH0[ph] + f + 1)
                nc.vector.tensor_tensor(a_lo[:, s, :], prod[:, s, :], a_hi[:, s, :].bitcast(F32),
                                        ALU.subtract).then_inc(al_done, 1)

            def ffn(ph, then=None):
                first, count = ADA_OF[ph]
                if ph != FFN0:
                    norm(ph)
                    rest_down(D0[ph], 0)

                def period(f, s, ada):
                    hidden(ph, f, s)
                    if ada is not None:
                        ada_half(*ada)
                    rest_up(U0[ph] + f + 2, s)
                    rest_down(D0[ph] + f + 1, 1 - s)

                def pair_of_periods(i):
                    even, odd = ada_beside(ph, i)
                    period(2 * i, 0, even)
                    period(2 * i + 1, 1, odd)
                last = NF // 2 - 1
                stop = min(last, count) if count else last
                pair_of_periods(0)
                with dve.Fori(1, stop) as i:
                    pair_of_periods(i)
                for i in range(stop, last):
                    pair_of_periods(i)
                period(NF - 2, 0, ada_beside(ph, last)[0])
                gate_column(ph)
                if then:
                    prepare(*then)
                hidden(ph, NF - 1, 1)
                add_output(ph)
                rest_up(U0[ph] + NF + 1, 1)


            nc.vector.memset(cv_u[:, :, 0:2], 0.0).then_inc(cv_pad, 1)
            dve.wait_ge(cols_in, 16)
            dve.wait_ge(pos_in, 16)
            two_pi = 2 * math.pi
            part1 = 6.28125
            part2 = float(np.float32(round((two_pi - part1) * 2 ** 19) / 2 ** 19))
            part3 = float(np.float32(two_pi - part1 - part2))
            magic = 1.5 * 2 ** 23
            steps = [0]

            def angle(ins):
                ins.then_inc(tab_step, 1)
                steps[0] += 1
                dve.wait_ge(tab_step, steps[0])
            angle(nc.vector.tensor_scalar(ang[:, 0, :], pos[:, :], col("inv_freq"), None, ALU.mult))
            angle(nc.vector.tensor_scalar(ang[:, 1, :], ang[:, 0, :], 1 / two_pi, magic, ALU.mult, ALU.add))
            angle(nc.vector.tensor_scalar(ang[:, 1, :], ang[:, 1, :], magic, None, ALU.subtract))
            for part in (part1, part2, part3):
                angle(nc.vector.scalar_tensor_tensor(out=ang[:, 0, :], in0=ang[:, 1, :], scalar=-part, in1=ang[:, 0, :],
                                                     op0=ALU.mult, op1=ALU.add))
            pi = float(np.nextafter(np.float32(math.pi), np.float32(0)))
            angle(nc.vector.tensor_scalar(ang[:, 0, :], ang[:, 0, :], pi, -pi, ALU.min, ALU.max))
            angle(nc.vector.scalar_tensor_tensor(out=ang[:, 1, :], in0=ang[:, 0, :], scalar=-1.0, in1=ang[:, 0, :],
                                                 op0=ALU.mult, op1=ALU.max))

            dve.wait_ge(c_done, 1)

            def start_half(i, between=None):
                slot, landed = start_slots[i % 4]
                dve.wait_ge(landed, 16 * (i // 4 + 1))
                for k in range(AH):
                    ada_sum(slot, i % 4, k, i, depth=4)
                    if between and k == 0:
                        between()
                keep(i % 4, AH * start_halves[i], i + 1)

            for i in range(4):
                start_half(i)
            dve.wait_ge(mod_done, KC)
            scale_column(FFN0)
            scaled(FFN0)
            for i in (4, 5):
                start_half(i)
            rest_up(0, 0)
            for j in range(4):
                shifted_rest(FFN0, j)
            start_half(6)
            start_half(7, between=lambda: [shifted_rest(FFN0, j) for j in (4, 5)])
            for j in (6, 7):
                shifted_rest(FFN0, j)
            rest_up(1, 1)
            rest_down(0, 0)
            ffn(FFN0, then=(ATTN, N_ADA_START + 8))

            rope = [0]

            def rotate(n, gain, dst):
                def step(ins):
                    ins.then_inc(rope_step, 1)
                    rope[0] += 1
                dve.wait_ge(head_rstd, 2 * n + 2)
                for t in range(2):
                    step(nc.vector.scalar_tensor_tensor(out=qk_n[:, t * T:(t + 1) * T], in0=qk_t[:, t * T:(t + 1) * T],
                                                        scalar=gain[:, t:t + 1], in1=qk_r[:, :],
                                                        op0=ALU.mult, op1=ALU.mult))
                dve.wait_ge(rope_step, rope[0])
                step(nc.vector.tensor_tensor(qk_c[:, :], qk_n[:, :], cos2[:, :], ALU.mult))
                step(nc.vector.tensor_tensor(qk_s[:, :], qk_n[:, :], sin2[:, :], ALU.mult))
                dve.wait_ge(rope_step, rope[0])
                if dst is not k_rot:
                    step(nc.vector.tensor_tensor(dst[:, 0:T], qk_c[:, 0:T], qk_s[:, T:2 * T], ALU.subtract))
                    nc.vector.tensor_tensor(dst[:, T:2 * T], qk_c[:, T:2 * T], qk_s[:, 0:T],
                                            ALU.add).then_inc(rot_done, 1)
                    return
                dve.wait_ge(k_zero, 1)
                for g in range(KV):
                    rows = slice(g * HALF, (g + 1) * HALF)
                    first = nc.vector.tensor_tensor(k_rot[rows, g, :], qk_c[rows, 0:T], qk_s[rows, T:2 * T],
                                                    ALU.subtract)
                    second = nc.vector.tensor_tensor(k_rot[rows, KV + g, :], qk_c[rows, T:2 * T], qk_s[rows, 0:T],
                                                     ALU.add)
                step(first)
                second.then_inc(rot_done, 1)

            def softmax_columns(r):
                s = r % 2
                for g in range(KV):
                    dve.wait_ge(scored, KV * r + g + 1)
                    nc.vector.scalar_tensor_tensor(out=probs[:, s, g, :], in0=s_bank(r, g)[:, 0:S_COLS],
                                                   scalar=HD ** -0.5,
                                                   in1=mask[:, :], op0=ALU.mult, op1=ALU.add).then_inc(masked, 1)
                    dve.wait_ge(masked, KV * r + g + 1)
                    nc.vector.tensor_reduce(m_col[:, s, g:g + 1], probs[:, s, g, 0:P], AX.X,
                                            ALU.max).then_inc(soft_step, 1)
                    nc.vector.tensor_reduce(m_col[:, s, KV + g:KV + g + 1], probs[:, s, g, P:S_COLS], AX.X,
                                            ALU.max).then_inc(soft_step, 1)
                dve.wait_ge(soft_step, SOFT * r + 2 * KV)
                sink = col("sinks", r * 2 * KV, 2 * KV)
                nc.vector.tensor_tensor(m_col[:, s, :], m_col[:, s, :], sink, ALU.max).then_inc(soft_step, 1)
                dve.wait_ge(soft_step, SOFT * r + 2 * KV + 1)
                nc.vector.tensor_scalar(nm_col[:, s, :], m_col[:, s, :], -1.0, None, ALU.mult).then_inc(soft_step, 1)
                nc.vector.tensor_tensor(sd_col[:, s, :], sink, m_col[:, s, :], ALU.subtract).then_inc(soft_step, 1)

            def normalise(r, h):
                s = r % 2

                def heads(c):
                    return c[:, s, :].rearrange("p (b g) -> p b g", b=2)[:, :, 2 * h:2 * h + 2]
                dve.wait_ge(exp_done, 9 * r + 1 + 4 * (h + 1))
                column(nc.vector.tensor_tensor(heads(de_col), heads(su_col), heads(es_col), ALU.add))
                column(nc.vector.reciprocal(heads(ri_col), heads(de_col)))
                for g in (2 * h, 2 * h + 1):
                    for b in range(2):
                        e = probs[:, s, g, 0:P] if b == 0 else probs[:, s, g, P:S_COLS]
                        nc.vector.tensor_scalar(e, e, ri_col[:, s, b * KV + g:b * KV + g + 1], None,
                                                ALU.mult).then_inc(norm_done, 1)

            def rest_output(t):
                dve.wait_ge(oh_done, t + 1)
                nc.vector.tensor_tensor(o_lo[:, t, :], o_bank[t % 2][:, 0:T], o_hi[:, t, :].bitcast(F32),
                                            ALU.subtract).then_inc(ol_done, 1)

            norm(ATTN)
            dve.wait_ge(consts_in, 16 * N_CONST_DMAS)
            rest_down(D0[ATTN], 0)
            rest_up(U0[ATTN] + 2, 0)
            dve.wait_ge(up_done, U0[ATTN] + 2)
            for b in range(2):
                nc.vector.tensor_tensor(v_sb[:, b, :], pair[1][:, b * T:(b + 1) * T], bv[:, :],
                                        ALU.add).then_inc(v_done, 1)
            rest_up(U0[ATTN] + 3, 1)
            rotate(0, col("k_gain"), k_rot)
            rest_up(U0[ATTN] + 4, 0)
            rotate(1, col("q_gain"), q_rot[:, 0, :])
            rest_up(U0[ATTN] + 5, 1)
            for r in range(GROUP):
                softmax_columns(r)
                if r < GROUP - 1:
                    rotate(r + 2, col("q_gain"), q_rot[:, (r + 1) % 2, :])
                    if r == 0:
                        ada_half(ADA_ATTN - 1, 1)
                for h in range(2):
                    if r:
                        rest_output(2 * (r - 1) + h)
                    normalise(r, h)
            rest_down(D0[ATTN] + 1, 1)
            for n in range(2):
                rest_up(U0[FFN1] + n, n)
            for t in (KC - 2, KC - 1):
                rest_output(t)
            for t in range(KC - 2):
                rest_down(D0[ATTN] + t + 2, t % 2)
                if t < AC:
                    ada_chunk(ADA_ATTN, t // AH, t % AH)
                elif t == AC:
                    prepare(FFN1, ADA_ATTN + 1)
                    gate_column(ATTN)
                    column(nc.vector.tensor_tensor(gb_col[:, :], mod_cols(0, 5), col("b_o"), ALU.mult))
                if t >= AC:
                    for j in range(4 * (t - AC), 4 * (t - AC) + 4):
                        ins = nc.vector.tensor_scalar(x[:, j, :], x[:, j, :], gb_col[:, j:j + 1], None, ALU.add)
                    column(ins)
            add_output(ATTN)

            ffn(FFN1, then=(FFN2, 22))
            ffn(FFN2, then=(CONV, ADA_OF[FFN3][0]))

            norm(CONV)
            rest_down(D0[CONV], 0)
            for i in range(KC // 2):
                def conv(s):
                    j = 2 * i + s
                    u = cv_u[:, s, :]
                    dve.wait_ge(cv_c, j + 1)
                    n = 10 * i + 5 * s
                    nc.vector.tensor_tensor(u[:, 2:2 + T], gate_s[:, s, :], pair[(3 * i + s) % 2][:, T:2 * T],
                                            ALU.mult).then_inc(cv_in, 1)
                    dve.wait_ge(cv_in, j + 1)
                    for w in range(3):
                        tap = col("conv_w", w * KC + j, 1)
                        if w == 0:
                            nc.vector.tensor_scalar(prod[:, s, :], u[:, 0:T], tap, None, ALU.mult).then_inc(cv_step, 1)
                        else:
                            dve.wait_ge(cv_step, n0[0])
                            nc.vector.scalar_tensor_tensor(out=prod[:, s, :], in0=u[:, w:w + T], scalar=tap,
                                                           in1=prod[:, s, :], op0=ALU.mult, op1=ALU.add).then_inc(cv_step, 1)
                        n0[0] += 1
                n0 = [10 * i]
                conv(0)
                rest_up(U0[CONV] + 3 * i + 2, (3 * i + 2) % 2)
                if i:
                    rest_down(D0[CONV] + 2 * i - 1, 1)
                conv(1)
                if i < KC // 2 - 1:
                    rest_up(U0[CONV] + 3 * i + 3, (3 * i + 3) % 2)
                dve.wait_ge(up_done, U0[CONV] + 3 * i + 3)
                dve.wait_ge(cv_step, n0[0])
                for s in range(2):
                    nc.vector.tensor_tensor(cv_y[:, s, :], prod[:, s, :], pair[(3 * i + 2) % 2][:, s * T:(s + 1) * T],
                                            ALU.mult).then_inc(cv_step, 2)
                    n0[0] += 2
                for s in range(2):
                    dve.wait_ge(ah_done, AH0[CONV] + 2 * i + s + 1)
                    nc.vector.tensor_tensor(o_lo[:, 2 * i + s, :], cv_y[:, s, :], o_hi[:, 2 * i + s, :].bitcast(F32),
                                            ALU.subtract).then_inc(al_done, 1)
                if i < KC // 2 - 1:
                    rest_up(U0[CONV] + 3 * i + 4, (3 * i + 4) % 2)
                if i:
                    rest_down(D0[CONV] + 2 * i, 0)
            rest_down(D0[CONV] + KC - 1, 1)
            gate_column(CONV)
            prepare(FFN3, ADA_UNITS)
            rest_up(U0[FFN3], 0)
            add_output(CONV)
            rest_up(U0[FFN3] + 1, 1)
            ffn(FFN3)

        @block.gpsimd
        def _(pool):
            pool.wait_ge(h_done, (ATTN + 1) * KC)
            nc.gpsimd.memset(k_rot[:, :, :], 0.0).then_inc(k_zero, 1)

        @block.tensor
        def _(pe):
            SQUARES_FROM = 5

            def keep_warm(times, bank=aux):
                for _ in range(times):
                    nc.tensor.matmul(bank[:, 0:T], mean_w[:, :], cos2[:, 0:T], start=True, stop=True)

            def three(out, w_hi, w_lo, m_hi, m_lo, start, stop):
                nc.tensor.matmul(out, w_hi, m_hi, start=start, stop=False, skip_group_check=True)
                nc.tensor.matmul(out, w_hi, m_lo, start=False, stop=False, skip_group_check=True)
                return nc.tensor.matmul(out, w_lo, m_hi, start=False, stop=stop, skip_group_check=True)

            def up(ph, f, s, first=False, ahead=False, begun=False):
                if ahead:
                    pe.wait_ge(up_hi_done, U0[ph] + f + 2)
                if first and ph == FFN0:
                    pe.wait_ge(tab_done, 4)
                    pe.wait_ge(up_hi_done, 1)
                    keep_warm(3)
                pe.wait_ge(up_lo_done, U0[ph] + f + 1)
                for k in range(KC):
                    if first and ph == FFN0 and k == KC // 2:
                        keep_warm(4)
                    tiles = [(pair[s][:, c * T:(c + 1) * T], (2 * k + c) * P) for c in range(2)]
                    if first:
                        pe.wait_ge(hh_done, ph * KC + k + 1)
                        for c, (out, at) in enumerate(tiles):
                            for w in (up_hi, up_lo):
                                nc.tensor.matmul(out, w[:, s, at:at + P], h_hi[:, k, :],
                                                 start=k == 0 and c == 0 and w is up_hi, stop=False,
                                                 skip_group_check=True)
                        if ahead:
                            for c, (_, at) in enumerate(tiles):
                                nc.tensor.matmul(pair[1 - s][:, c * T:(c + 1) * T], up_hi[:, 1 - s, at:at + P],
                                                 h_hi[:, k, :], start=k == 0 and c == 0, stop=False,
                                                 skip_group_check=True)
                        pe.wait_ge(h_done, ph * KC + k + 1)
                    for c, (out, at) in enumerate(tiles):
                        if first:
                            ins = nc.tensor.matmul(out, up_hi[:, s, at:at + P], h_lo[:, k, :],
                                                   start=False, stop=k == KC - 1, skip_group_check=True)
                        elif begun:
                            nc.tensor.matmul(out, up_hi[:, s, at:at + P], h_lo[:, k, :], start=False, stop=False,
                                             skip_group_check=True)
                            ins = nc.tensor.matmul(out, up_lo[:, s, at:at + P], h_hi[:, k, :],
                                                   start=False, stop=k == KC - 1, skip_group_check=True)
                        else:
                            ins = three(out, up_hi[:, s, at:at + P], up_lo[:, s, at:at + P],
                                        h_hi[:, k, :], h_lo[:, k, :], k == 0 and c == 0, k == KC - 1)
                ins.then_inc(up_done, 1)

            def square_sum(ph, j):
                pe.wait_ge(sq_done, ph * KC + j + 1)
                ins = nc.tensor.matmul(stat[:, 0:T], mean_w[:, :], sq[:, j, :], start=j == 0, stop=j == KC - 1)
                if j == KC - 1:
                    ins.then_inc(mean_done, 1)

            def down(n, s, m_hi, m_lo, first=False, last=False, then=None):
                pe.wait_ge(dn_lo_done, n + 1)
                for j in range(KC):
                    ins = three(acc[j // 2][:, (j % 2) * T:(j % 2 + 1) * T], dn_hi[:, s, j * P:(j + 1) * P],
                                dn_lo[:, s, j * P:(j + 1) * P], m_hi, m_lo, first and j % 2 == 0, last)
                    if last and j % 2 and j < KC - 1:
                        ins.then_inc(bank_done, 1)
                    if last and j == KC - 1:
                        ins.then_inc(dn_done, 1)
                    if then is not None and j >= SQUARES_FROM:
                        square_sum(then, j - SQUARES_FROM)
                if not last:
                    ins.then_inc(dn_done, 1)
                if then is not None:
                    for j in range(KC - SQUARES_FROM, KC):
                        square_sum(then, j)
                    keep_warm(4)

            def ffn(ph, then=None):
                def up_f(f, s):
                    if not isinstance(f, int) or f >= 2:
                        pe.wait_ge(prod_done, FFN_NUMBER[ph] * NF + f - 1)
                    at = f if isinstance(f, int) else -1
                    up(ph, f, s, first=at == 0, ahead=at == 0 and ph != FFN0, begun=at == 1 and ph != FFN0)

                def down_f(f, s, **kw):
                    pe.wait_ge(al_done, AH0[ph] + f + 1)
                    down(D0[ph] + f, s, a_hi[:, s, :], a_lo[:, s, :], **kw)

                up_f(0, 0)
                up_f(1, 1)
                down_f(0, 0, first=True)
                with pe.Fori(1, NF // 2 - 1) as i:
                    up_f(2 * i, 0)
                    down_f(2 * i - 1, 1)
                    up_f(2 * i + 1, 1)
                    down_f(2 * i, 0)
                up_f(NF - 2, 0)
                down_f(NF - 3, 1)
                up_f(NF - 1, 1)
                down_f(NF - 2, 0)
                down_f(NF - 1, 1, last=True, then=then)

            pe.wait_ge(mean_w_in, 16)
            for j in range(KC):
                square_sum(FFN0, j)
            ffn(FFN0, then=ATTN)
            pe.wait_ge(consts_in, 16 * N_CONST_DMAS)

            def head_norm(n):
                pe.wait_ge(squared, n + 1)
                if n:
                    pe.wait_ge(head_rstd, 2 * n - 1)
                for t in range(2):
                    ins = nc.tensor.matmul(stat[:, 0:T], head_w[:, :], qk_sq[:, t * T:(t + 1) * T],
                                           start=t == 0, stop=t == 1)
                ins.then_inc(head_mean, 1)

            def scores(r):
                pe.wait_ge(rot_done, r + 2)
                q = q_rot[:, r % 2, :]
                for g in range(KV):
                    n = KV * r + g
                    if g == 0 and r:
                        pe.wait_ge(masked, n)
                    elif g == 2 and r == 2:
                        pe.wait_ge(biased, 2 * GROUP + 2)
                    elif g == KV - 1:
                        pe.wait_ge(masked, n - 2)
                    for b in range(2):
                        out = s_bank(r, g)[:, b * P:S_COLS if b else P]
                        for t in range(2):
                            ins = nc.tensor.matmul(out, q[:, t * T + b * P:t * T + (b + 1) * P],
                                                   k_rot[:, t * KV + g, 0:(b + 1) * P],
                                                   start=t == 0, stop=t == 1)
                    ins.then_inc(scored, 1)

            def turn(r, g):
                n = KV * r + g
                pe.wait_ge(norm_done, 2 * n + 2)
                if n >= 2:
                    pe.wait_ge(pt_done, n - 1)
                for c in range(3):
                    ins = nc.tensor.transpose(acc[2 + g % 2][:, c * P:(c + 1) * P],
                                              probs[:, r % 2, g, c * P:(c + 1) * P], ident[:, :])
                ins.then_inc(pt_ready, 1)

            def weigh(r, g):
                n = KV * r + g
                pe.wait_ge(pt_done, n + 1)
                if n == 0:
                    pe.wait_ge(v_done, 2)
                    pe.wait_ge(masked, 2 * KV)
                t = n // 2
                if g % 2 == 0 and t >= 2:
                    pe.wait_ge(ol_done, t - 1)
                rows = slice((g % 2) * HD, (g % 2 + 1) * HD)
                for b, c, start, stop in ((0, 0, True, True), (0, 1, True, False), (1, 2, False, True)):
                    q = 0 if c == 0 else P
                    ins = nc.tensor.matmul(o_bank[t % 2][rows, q:q + P], v_sb[:, b, g * HD:(g + 1) * HD],
                                           p_t[:, g % 2, c * P:(c + 1) * P], start=start, stop=stop)
                ins.then_inc(pv_done, 1)

            def heads(r):
                if r == GROUP - 1:
                    pe.wait_ge(head_rstd, 2 * GROUP + 1)
                    keep_warm(3, stat)
                turn(r, 0)
                turn(r, 1)
                if r < GROUP - 2:
                    head_norm(r + 3)
                for g in range(KV):
                    if 0 < g < KV - 1:
                        turn(r, g + 1)
                    weigh(r, g)

            up(ATTN, 0, 0, True)
            pe.wait_ge(up_lo_done, U0[ATTN] + 2)
            for b in range(2):
                for k in range(KC):
                    at = 2 * k * P
                    blk = slice(b * P, (b + 1) * P)
                    out = pair[1][:, b * T:(b + 1) * T]
                    nc.tensor.matmul(out, h_hi[:, k, blk], up_hi[:, 1, at:at + T], start=k == 0, stop=False,
                                     skip_group_check=True)
                    nc.tensor.matmul(out, h_lo[:, k, blk], up_hi[:, 1, at:at + T], start=False, stop=False,
                                     skip_group_check=True)
                    ins = nc.tensor.matmul(out, h_hi[:, k, blk], up_lo[:, 1, at:at + T], start=False, stop=k == KC - 1,
                                           skip_group_check=True)
                if b == 0:
                    head_norm(0)
            ins.then_inc(up_done, 1)
            pe.wait_ge(biased, 2)
            up(ATTN, 2, 0)
            pe.wait_ge(v_done, 2)
            up(ATTN, 3, 1)
            head_norm(1)
            pe.wait_ge(biased, 4)
            up(ATTN, 4, 0)
            for r in range(GROUP):
                scores(r)
                if r == 0:
                    head_norm(2)
                    pe.wait_ge(biased, 6)
                    up(ATTN, 5, 1)
                else:
                    heads(r - 1)
            heads(GROUP - 1)
            pe.wait_ge(masked, KV * GROUP)
            pe.wait_ge(pt_done, KV * GROUP)
            for t in range(KC):
                pe.wait_ge(ol_done, t + 1)
                down(D0[ATTN] + t, t % 2, o_hi[:, t, :], o_lo[:, t, :], first=t == 0, last=t == KC - 1,
                     then=FFN1 if t == KC - 1 else None)

            ffn(FFN1, then=FFN2)
            ffn(FFN2, then=CONV)

            def down_pair(i):
                for s in range(2):
                    t = 2 * i + s
                    pe.wait_ge(al_done, AH0[CONV] + t + 1)
                    down(D0[CONV] + t, s, o_hi[:, t, :], o_lo[:, t, :], first=t == 0, last=t == KC - 1,
                         then=FFN3 if t == KC - 1 else None)
            for i in range(KC // 2):
                for s in range(3):
                    u = 3 * i + s
                    if u >= 2:
                        v = u - 2
                        if v % 3 == 2:
                            pe.wait_ge(cv_step, 10 * (v // 3) + 10)
                        else:
                            pe.wait_ge(cv_in, 2 * (v // 3) + v % 3 + 1)
                    up(CONV, u, u % 2, first=u == 0, ahead=u == 0, begun=u == 1)
                if i:
                    down_pair(i - 1)
            down_pair(KC // 2 - 1)
            ffn(FFN3)


AH0 = {FFN0: 0, FFN1: NF, FFN2: 2 * NF, CONV: 3 * NF, FFN3: 3 * NF + KC}


def kernel(x, c, positions, norm_gain, w_ada, b_ada, w_ffn_up, w_ffn_down, attn_w_qkv, attn_b_qkv,
           attn_q_gain, attn_k_gain, attn_sinks, attn_w_o, attn_b_o, conv_w_in, conv_w, conv_w_out):
    import concourse.bacc as bacc
    from concourse.bass_utils import run_bass_kernel_spmd as run

    f32 = np.float32

    def chunks(v):
        return np.asarray(v).reshape(-1, KC, P).transpose(2, 0, 1).reshape(P, -1)

    bq = np.asarray(attn_b_qkv)[0, :HEADS * HD].reshape(KV, GROUP, 2, HALF)
    bk = np.asarray(attn_b_qkv)[0, HEADS * HD:(HEADS + KV) * HD].reshape(KV, 2, HALF)
    v_at = (HEADS + KV) * HD

    def per_half(g):
        return np.broadcast_to(np.asarray(g)[0].reshape(1, 2, HALF).transpose(0, 2, 1), (KV, HALF, 2)).reshape(P, 2)

    sinks = np.asarray(attn_sinks)[0].reshape(KV, GROUP).transpose(1, 0)
    sinks = np.broadcast_to(sinks[None, :, None, :], (P, GROUP, 2, KV)).reshape(P, -1)
    inv = (f32(10000.0) ** (-np.arange(0, HD, 2, dtype=f32) / f32(HD))).astype(f32)
    parts = {
        "gain": chunks(norm_gain), "b_ada": chunks(b_ada), "conv_w": chunks(conv_w), "b_o": chunks(attn_b_o),
        "b_q": bq.transpose(0, 3, 1, 2).reshape(P, -1), "b_k": bk.transpose(0, 2, 1).reshape(P, -1),
        "q_gain": per_half(attn_q_gain), "k_gain": per_half(attn_k_gain), "sinks": sinks,
        "inv_freq": np.tile(inv, KV)[:, None], "half_pi": np.full((P, 1), math.pi / 2, f32),
        "eps": np.full((P, 1), EPS, f32),
    }
    cols = np.concatenate([parts[n] for n in COLS], axis=1)
    q = np.arange(P)[:, None]
    mask = np.zeros((P, S_COLS), f32)
    mask[:, :P][q < np.arange(P)[None]] = MASKED
    rel = P + q - np.arange(2 * P)[None]
    mask[:, P:][(rel < 0) | (rel >= P)] = MASKED
    w_qkv = np.asarray(attn_w_qkv)[0].reshape(KC, P, -1)
    wq = w_qkv[:, :, :HEADS * HD].reshape(KC, P, KV, GROUP, 2, HALF).transpose(3, 1, 0, 4, 2, 5).reshape(GROUP, P, UP)
    wk = w_qkv[:, :, HEADS * HD:v_at].reshape(KC, P, KV, 2, HALF).transpose(1, 0, 3, 2, 4).reshape(1, P, UP)
    wv = w_qkv[:, :, v_at:].transpose(1, 0, 2).reshape(1, P, UP)
    w_in = np.asarray(conv_w_in)[0].reshape(KC, P, 3, KC // 2, 2, P)
    cv = w_in[:, :, 1:].transpose(3, 4, 1, 0, 2, 5).reshape(KC // 2, 2, P, UP)
    gb = w_in[:, :, 0].transpose(2, 1, 0, 3, 4).reshape(KC // 2, 1, P, UP)
    arrays = {
        "x_t": np.asarray(x)[0].T,
        "c_d": np.asarray(c)[0],
        "cols_d": cols,
        "pos_d": np.asarray(positions)[0],
        "bv_d": np.asarray(attn_b_qkv)[0, v_at:],
        "ident_d": np.eye(P, dtype=f32),
        "ones_d": np.full((P, P), 1 / D, f32),
        "heads_d": np.kron(np.eye(KV, dtype=f32), np.full((HALF, HALF), 1 / HD, f32)),
        "mask_d": mask,
        "w_ada_d": np.asarray(w_ada).reshape(2, D, -1, AH, P).transpose(0, 2, 4, 3, 1).reshape(-1, P, AH * D),
        "w_up_d": np.asarray(w_ffn_up).reshape(4, KC, P, 2, NF, P).transpose(0, 4, 2, 1, 3, 5).reshape(-1, P, UP),
        "w_down_d": np.asarray(w_ffn_down).reshape(-1, P, DN),
        "w_qkv_d": np.concatenate([wk, wv, wq]),
        "w_o_d": np.asarray(attn_w_o)[0].reshape(2, 2, GROUP, HD, D).transpose(2, 0, 1, 3, 4).reshape(KC, P, D),
        "w_cin_d": np.concatenate([cv, gb], axis=1).reshape(-1, P, UP),
        "w_cout_d": np.asarray(conv_w_out)[0].reshape(KC, P, D),
    }
    arrays = {n: np.ascontiguousarray(a) for n, a in arrays.items()}
    nc = bacc.Bacc("TRN2", target_bir_lowering=False, num_devices=1)
    aps = [nc.dram_tensor(n, a.shape, mybir.dt.from_np(a.dtype), kind="ExternalInput").ap() for n, a in arrays.items()]
    aps.append(nc.dram_tensor("out_t", (D, T), F32, kind="ExternalOutput").ap())
    build(nc, *aps)
    r = run(nc, [arrays], core_ids=[0])
    return r.results[0]["out_t"].T.reshape(1, T, D)
```
